# Optimizing a Trainium2 kernel written in Bass

```python
import math
import jax, jax.numpy as jnp
from jax import lax
import numpy as np

D_MODEL = 1024
BATCH = 1
SEQ = 128
DEPTH = 2
DEC_BATCH = 1
DEC_SEQ = 512
PAST_LEN = 128

GRID_W = 64
HEAD_DIM = 64
GQA_Q_HEADS = 4
GQA_KV_HEADS = 2
D_GQA_Q = GQA_Q_HEADS * HEAD_DIM
D_GQA_KV = GQA_KV_HEADS * HEAD_DIM
POOL_WINDOWS = (2, 4, 8, 16)
POOL_GROUP_W = 64
D_POOL = POOL_GROUP_W * len(POOL_WINDOWS)
D_CONV = 256
CONV_WIDTH = 31
DIFF_HEADS = 4
D_DIFF = DIFF_HEADS * HEAD_DIM
DIFF_LAMBDA_DIM = HEAD_DIM // 2
D_MIX = D_GQA_Q + D_POOL + D_CONV + D_DIFF
PROJ_SIZES = (D_GQA_Q, D_GQA_KV, D_GQA_KV, D_POOL, 2 * D_CONV, D_DIFF, D_DIFF, D_DIFF)
SPLIT_POINTS = (256, 384, 512, 768, 1280, 1536, 1792)
D_IN_PROJ = 2048
N_EXPERTS = 16
EXPERT_FF = 1024
EC_CAPACITY_FACTOR = 2
N_MOD = 6
Q_BLOCK = 128
ROPE_BASE = 10000.0
EPS = 1e-6

kernel_name = "hybrid_dit_prefix_ctx_step"

F32 = jnp.float32

def _rms(x, g):
    xf = x.astype(F32)
    y = xf * lax.rsqrt(jnp.mean(xf * xf, axis=-1, keepdims=True) + EPS)
    return (y * g.astype(F32)).astype(x.dtype)

def _axial_rope_tables(n_tok, dim):
    rows = n_tok // GRID_W
    row = jnp.repeat(jnp.arange(rows), GRID_W).astype(F32)
    col = jnp.tile(jnp.arange(GRID_W), rows).astype(F32)
    quarter = dim // 4
    inv = ROPE_BASE ** (-jnp.arange(quarter, dtype=F32) / quarter)
    ang = jnp.concatenate([row[:, None] * inv, col[:, None] * inv], axis=-1)
    return jnp.cos(ang), jnp.sin(ang)

def _apply_rope(x, cos, sin):
    xf = x.astype(F32).reshape(*x.shape[:-1], x.shape[-1] // 2, 2)
    x1, x2 = xf[..., 0], xf[..., 1]
    cs, sn = cos[None, :, None, :], sin[None, :, None, :]
    out = jnp.stack([x1 * cs - x2 * sn, x1 * sn + x2 * cs], axis=-1).reshape(x.shape)
    return out.astype(x.dtype)

def _map_q_blocks(fn, q):
    b, lq = q.shape[:2]
    nb = lq // Q_BLOCK
    blocks = jnp.moveaxis(q.reshape(b, nb, Q_BLOCK, *q.shape[2:]), 1, 0)
    out = lax.map(fn, blocks)
    return jnp.moveaxis(out, 0, 1).reshape(b, lq, *out.shape[3:])

def _gqa_attend(q, k, v):
    hq, dh = q.shape[2], q.shape[3]
    hkv = k.shape[2]
    rep = hq // hkv
    scale = dh ** -0.5

    def blk(qb):
        qg = qb.reshape(qb.shape[0], qb.shape[1], hkv, rep, dh)
        s = jnp.einsum('bqgrd,bkgd->bgrqk', qg, k).astype(F32) * scale
        p = jax.nn.softmax(s, axis=-1).astype(v.dtype)
        o = jnp.einsum('bgrqk,bkgd->bqgrd', p, v)
        return o.reshape(qb.shape[0], qb.shape[1], hq * dh)

    return _map_q_blocks(blk, q)

def _diff_attend(q, k, v, lam):
    d = q.shape[-1] // 2
    scale = d ** -0.5
    k1, k2 = k[..., :d], k[..., d:]

    def blk(qb):
        s1 = jnp.einsum('bqhd,bkhd->bhqk', qb[..., :d], k1).astype(F32) * scale
        s2 = jnp.einsum('bqhd,bkhd->bhqk', qb[..., d:], k2).astype(F32) * scale
        p = jax.nn.softmax(s1, axis=-1) - lam * jax.nn.softmax(s2, axis=-1)
        return jnp.einsum('bhqk,bkhd->bqhd', p.astype(v.dtype), v)

    return _map_q_blocks(blk, q)

def _multiscale_pool(x, pool_w, pool_scale):
    n = x.shape[1]
    xf = x.astype(F32)
    cs = jnp.concatenate([jnp.zeros_like(xf[:, :1]), jnp.cumsum(xf, axis=1)], axis=1)
    t = jnp.arange(n)
    outs = []
    for gi, w in enumerate(POOL_WINDOWS):
        sl = slice(gi * POOL_GROUP_W, (gi + 1) * POOL_GROUP_W)
        lo = jnp.maximum(t - w // 2, 0)
        hi = jnp.minimum(t + (w - w // 2) - 1, n - 1)
        cg = cs[..., sl]
        mean = (cg[:, hi + 1] - cg[:, lo]) / (hi - lo + 1).astype(F32)[None, :, None]
        outs.append((mean - xf[..., sl]).astype(x.dtype) @ pool_w[gi])
    return jnp.concatenate(outs, axis=-1) * pool_scale

def _conformer_conv(g_in, dw_w, dw_b, ln_g, ln_b, pw_w):
    a, gate = jnp.split(g_in, 2, axis=-1)
    u = a * jax.nn.sigmoid(gate)
    y = lax.conv_general_dilated(u, dw_w[:, None, :].astype(u.dtype), window_strides=(1,),
                                 padding=[(CONV_WIDTH // 2, CONV_WIDTH // 2)],
                                 dimension_numbers=('NWC', 'WIO', 'NWC'),
                                 feature_group_count=D_CONV) + dw_b
    yf = y.astype(F32)
    mu = jnp.mean(yf, axis=-1, keepdims=True)
    var = jnp.mean(jnp.square(yf - mu), axis=-1, keepdims=True)
    yn = (yf - mu) * lax.rsqrt(var + EPS) * ln_g.astype(F32) + ln_b.astype(F32)
    return jax.nn.silu(yn).astype(g_in.dtype) @ pw_w

def _mixing_sublayer(h, p, lam, lambda_init, rope, ctx_kv):
    b, n = h.shape[:2]
    u = h @ p['w_in']
    qa, ka, va, pool_in, glu_in, qd, kd, vd = jnp.split(u, SPLIT_POINTS, axis=-1)
    qa = _rms(qa.reshape(b, n, GQA_Q_HEADS, HEAD_DIM), p['gqa_qn_g'])
    ka = _rms(ka.reshape(b, n, GQA_KV_HEADS, HEAD_DIM), p['gqa_kn_g'])
    va = va.reshape(b, n, GQA_KV_HEADS, HEAD_DIM)
    qd = qd.reshape(b, n, DIFF_HEADS, HEAD_DIM)
    kd = kd.reshape(b, n, DIFF_HEADS, HEAD_DIM)
    vd = vd.reshape(b, n, DIFF_HEADS, HEAD_DIM)
    own = (ka, va, kd, vd)
    if rope is None:
        ka_all, va_all, kd_all, vd_all = ka, va, kd, vd
    else:
        cos64, sin64, cos32, sin32 = rope
        dl = DIFF_LAMBDA_DIM
        qa = _apply_rope(qa, cos64, sin64)
        ka_r = _apply_rope(ka, cos64, sin64)
        qd = jnp.concatenate([_apply_rope(qd[..., :dl], cos32, sin32), _apply_rope(qd[..., dl:], cos32, sin32)], axis=-1)
        kd_r = jnp.concatenate([_apply_rope(kd[..., :dl], cos32, sin32), _apply_rope(kd[..., dl:], cos32, sin32)], axis=-1)
        ck_a, cv_a, ck_d, cv_d = ctx_kv
        ka_all = jnp.concatenate([ck_a, ka_r], axis=1)
        va_all = jnp.concatenate([cv_a, va], axis=1)
        kd_all = jnp.concatenate([ck_d, kd_r], axis=1)
        vd_all = jnp.concatenate([cv_d, vd], axis=1)
    o_a = _gqa_attend(qa, ka_all, va_all)
    o_b = _multiscale_pool(pool_in, p['pool_w'], p['pool_scale'])
    o_c = _conformer_conv(glu_in, p['conv_dw_w'], p['conv_dw_b'], p['conv_ln_g'],
                          p['conv_ln_b'], p['conv_pw_w'])
    o_d = _diff_attend(qd, kd_all, vd_all, lam)
    o_d = (_rms(o_d, p['diff_subln_g']) * (1.0 - lambda_init)).reshape(b, n, D_DIFF)
    out = jnp.concatenate([o_a, o_b, o_c, o_d], axis=-1) @ p['w_out']
    return out, own

def _expert_choice_ffn(h, router_w, wg, wu, wd):
    b, n, d = h.shape
    cap = EC_CAPACITY_FACTOR * n // N_EXPERTS
    aff = jax.nn.softmax(jnp.einsum('bnd,de->bne', h, router_w).astype(F32), axis=-1)
    gate, idx = lax.top_k(jnp.swapaxes(aff, 1, 2), cap)
    xe = jax.vmap(lambda hb, ib: hb[ib])(h, idx)
    hid = jax.nn.silu(jnp.einsum('becd,edf->becf', xe, wg)) * jnp.einsum('becd,edf->becf', xe, wu)
    ye = jnp.einsum('becf,efd->becd', hid, wd) * gate[..., None].astype(h.dtype)
    return jax.vmap(lambda ib, yb: jnp.zeros((n, d), h.dtype).at[ib.reshape(-1)].add(yb.reshape(-1, d)))(idx, ye)

def _layer(x, mod, p, lam, lambda_init, rope, ctx_kv):
    sh1, sc1, g1, sh2, sc2, g2 = jnp.split(mod, N_MOD, axis=-1)
    h = _rms(x, p['norm1_g']) * (1.0 + sc1) + sh1
    m, own = _mixing_sublayer(h, p, lam, lambda_init, rope, ctx_kv)
    x = x + g1 * m
    h2 = _rms(x, p['norm2_g']) * (1.0 + sc2) + sh2
    x = x + g2 * _expert_choice_ffn(h2, p['router_w'], p['exp_w_gate'], p['exp_w_up'], p['exp_w_down'])
    return x, own

def setup_inputs(seed: int = 0) -> dict:
    key = jax.random.key(seed)
    ks = iter(jax.random.split(key, 40))

    def nrm(shape, s=1.0):
        return jax.random.normal(next(ks), shape, F32) * s

    def gain(shape):
        return 1.0 + 0.01 * jax.random.normal(next(ks), shape, F32)

    D = D_MODEL
    return {
        'x_prompt': nrm((BATCH, SEQ, D)),
        'x_sample': nrm((DEC_BATCH, DEC_SEQ, D)),
        'c': nrm((DEC_BATCH, D)),
        'cache_gqa_k': nrm((DEC_BATCH, DEPTH, PAST_LEN, GQA_KV_HEADS, HEAD_DIM)),
        'cache_gqa_v': nrm((DEC_BATCH, DEPTH, PAST_LEN, GQA_KV_HEADS, HEAD_DIM)),
        'cache_diff_k': nrm((DEC_BATCH, DEPTH, PAST_LEN, DIFF_HEADS, HEAD_DIM)),
        'cache_diff_v': nrm((DEC_BATCH, DEPTH, PAST_LEN, DIFF_HEADS, HEAD_DIM)),
        'c_ctx': nrm((D,)),
        'w_mod': nrm((DEPTH, D, N_MOD * D), 0.5 * D ** -0.5),
        'b_mod': nrm((DEPTH, N_MOD * D), 0.01),
        'norm1_g': gain((DEPTH, D)),
        'w_in': nrm((DEPTH, D, D_IN_PROJ), D ** -0.5),
        'gqa_qn_g': gain((DEPTH, HEAD_DIM)),
        'gqa_kn_g': gain((DEPTH, HEAD_DIM)),
        'pool_w': nrm((DEPTH, len(POOL_WINDOWS), POOL_GROUP_W, POOL_GROUP_W), POOL_GROUP_W ** -0.5),
        'pool_scale': gain((DEPTH, D_POOL)),
        'conv_dw_w': nrm((DEPTH, CONV_WIDTH, D_CONV), CONV_WIDTH ** -0.5),
        'conv_dw_b': nrm((DEPTH, D_CONV), 0.01),
        'conv_ln_g': gain((DEPTH, D_CONV)),
        'conv_ln_b': nrm((DEPTH, D_CONV), 0.01),
        'conv_pw_w': nrm((DEPTH, D_CONV, D_CONV), D_CONV ** -0.5),
        'diff_lq1': nrm((DEPTH, DIFF_LAMBDA_DIM), 0.1),
        'diff_lk1': nrm((DEPTH, DIFF_LAMBDA_DIM), 0.1),
        'diff_lq2': nrm((DEPTH, DIFF_LAMBDA_DIM), 0.1),
        'diff_lk2': nrm((DEPTH, DIFF_LAMBDA_DIM), 0.1),
        'diff_subln_g': gain((DEPTH, HEAD_DIM)),
        'w_out': nrm((DEPTH, D_MIX, D), D_MIX ** -0.5),
        'norm2_g': gain((DEPTH, D)),
        'router_w': nrm((DEPTH, D, N_EXPERTS), D ** -0.5),
        'exp_w_gate': nrm((DEPTH, N_EXPERTS, D, EXPERT_FF), D ** -0.5),
        'exp_w_up': nrm((DEPTH, N_EXPERTS, D, EXPERT_FF), D ** -0.5),
        'exp_w_down': nrm((DEPTH, N_EXPERTS, EXPERT_FF, D), EXPERT_FF ** -0.5),
        'final_g': gain((D,)),
    }

def reference(x_prompt, x_sample, c, cache_gqa_k, cache_gqa_v, cache_diff_k, cache_diff_v, c_ctx,
              w_mod, b_mod, norm1_g, w_in, gqa_qn_g, gqa_kn_g, pool_w, pool_scale,
              conv_dw_w, conv_dw_b, conv_ln_g, conv_ln_b, conv_pw_w,
              diff_lq1, diff_lk1, diff_lq2, diff_lk2, diff_subln_g, w_out, norm2_g,
              router_w, exp_w_gate, exp_w_up, exp_w_down, final_g):
    n_lat = x_sample.shape[1]
    cos64, sin64 = _axial_rope_tables(n_lat, HEAD_DIM)
    cos32, sin32 = _axial_rope_tables(n_lat, DIFF_LAMBDA_DIM)
    rope = (cos64, sin64, cos32, sin32)
    xc, xs = x_prompt, x_sample
    ks_a, vs_a, ks_d, vs_d = [], [], [], []
    for l in range(DEPTH):
        p = {
            'w_in': w_in[l], 'gqa_qn_g': gqa_qn_g[l], 'gqa_kn_g': gqa_kn_g[l],
            'pool_w': pool_w[l], 'pool_scale': pool_scale[l],
            'conv_dw_w': conv_dw_w[l], 'conv_dw_b': conv_dw_b[l], 'conv_ln_g': conv_ln_g[l],
            'conv_ln_b': conv_ln_b[l], 'conv_pw_w': conv_pw_w[l], 'diff_subln_g': diff_subln_g[l],
            'w_out': w_out[l], 'norm1_g': norm1_g[l], 'norm2_g': norm2_g[l], 'router_w': router_w[l],
            'exp_w_gate': exp_w_gate[l], 'exp_w_up': exp_w_up[l], 'exp_w_down': exp_w_down[l],
        }
        lambda_init = 0.8 - 0.6 * math.exp(-0.3 * l)
        lam = (jnp.exp(jnp.sum((diff_lq1[l] * diff_lk1[l]).astype(F32)))
               - jnp.exp(jnp.sum((diff_lq2[l] * diff_lk2[l]).astype(F32))) + lambda_init)
        mod_ctx = (jax.nn.silu(c_ctx) @ w_mod[l] + b_mod[l])[None, None, :]
        mod_lat = (jax.nn.silu(c) @ w_mod[l] + b_mod[l])[:, None, :]
        xc, (ka, va, kd, vd) = _layer(xc, mod_ctx, p, lam, lambda_init, None, None)
        ks_a.append(ka)
        vs_a.append(va)
        ks_d.append(kd)
        vs_d.append(vd)
        ctx_kv = (cache_gqa_k[:, l], cache_gqa_v[:, l], cache_diff_k[:, l], cache_diff_v[:, l])
        xs, _ = _layer(xs, mod_lat, p, lam, lambda_init, rope, ctx_kv)
    y_prompt = _rms(xc, final_g)
    y_sample = _rms(xs, final_g)
    state_gqa_k = jnp.stack(ks_a, axis=1)
    state_gqa_v = jnp.stack(vs_a, axis=1)
    state_diff_k = jnp.stack(ks_d, axis=1)
    state_diff_v = jnp.stack(vs_d, axis=1)
    return (y_prompt, y_sample, state_gqa_k, state_gqa_v, state_diff_k, state_diff_v)


_drawn_inputs = setup_inputs


def setup_inputs(seed=0):
    import zlib

    import numpy as np

    out = dict(_drawn_inputs(seed))
    spreads = {}
    factors = {'cache_gqa_k': 7.765,
     'cache_gqa_v': 6.689,
     'b_mod': 3.723,
     'norm1_g': 5.608,
     'gqa_qn_g': 8.0,
     'gqa_kn_g': 5.474,
     'pool_scale': 8.0,
     'conv_dw_b': 8.0,
     'conv_ln_g': 48.485,
     'conv_ln_b': 46.461,
     'diff_lq1': 6.436,
     'diff_lk1': 5.199,
     'diff_lq2': 6.517,
     'diff_lk2': 5.571,
     'diff_subln_g': 36.933,
     'norm2_g': 8.0,
     'final_g': 30.226}
    for name, (base, spread) in spreads.items():
        noise = np.random.default_rng([zlib.crc32(name.encode()), seed]).standard_normal(out[name].shape)
        drawn = base * np.exp(spread * noise) if base else spread * noise
        out[name] = __import__('jax').numpy.asarray(drawn.astype(out[name].dtype))
    for name, factor in factors.items():
        out[name] = (out[name] * factor).astype(out[name].dtype)
    return out
```

```python
import concourse.bass as bass
from concourse import mybir
from contextlib import ExitStack

import numpy as np


def backbone_step_kernel(nc, ins, outs):
    F32, U32, BF16 = mybir.dt.float32, mybir.dt.uint32, mybir.dt.bfloat16
    ALU, ACT, AX = mybir.AluOpType, mybir.ActivationFunctionType, mybir.AxisListType

    P = 128
    D = 1024
    LAT, CTX = 512, 128
    TOK = LAT + CTX
    NT = TOK // P
    LT = LAT // P
    KD = D // P
    LAYERS = 2
    EXPERTS = 16
    CAPL, CAPC = 2 * LAT // EXPERTS, 2 * CTX // EXPERTS
    CAP = CAPL + CAPC
    HD = 64
    EPS = 1e-6
    TAPS, PAD = 31, 15
    SEQW = PAD + LAT + PAD + CTX + PAD
    CTX0 = PAD + LAT + PAD
    OUTW = SEQW - 2 * PAD
    ROUNDS = 3 + EXPERTS
    PHASES = 6

    ctx = ExitStack()
    with ctx:
        def sb(name, shape, dt=F32):
            return ctx.enter_context(nc.sbuf_tensor(name, shape, dt))

        def sem(name):
            return ctx.enter_context(nc.semaphore(name))

        ring = sb("ring", [P, 6, 4, D])
        H = sb("H", [P, KD, TOK])
        ident = sb("ident", [P, P])
        mean_w = sb("mean_w", [P, P])
        neghalf = sb("neghalf", [P, 1])
        rope_a = sb("rope_a", [P, LT, 2, HD])
        rope_d = sb("rope_d", [P, LT, 2, HD // 2])
        edge = sb("edge", [P, 2, 2, 8])
        invw = sb("invw", [P, 2])
        crow = sb("crow", [16, P])
        scT = sb("scT", [P, 2, KD])
        prow = sb("prow", [24, P])
        pT = sb("pT", [P, 24])
        cwrow = sb("cwrow", [TAPS, 2 * P])
        cwT = sb("cwT", [P, 2, 32])
        head_g = sb("head_g", [P, 3, HD])
        subg = sb("subg", [P, HD])
        lamv = sb("lamv", [P, 4, 32])
        lamc = sb("lamc", [P, 2])
        lamw = sb("lamw", [P, 2, 32])
        lams = sb("lams", [P, 8])
        router = sb("router", [P, KD, EXPERTS])
        pool_w = sb("pool_w", [P, 2, P])
        conv_pw = sb("conv_pw", [P, 2, 2 * P])
        ck = sb("ck", [P, 384])
        cv = sb("cv", [P, 384])
        kcT = sb("kcT", [P, 3, P])
        modA = sb("modA", [P, 2, 2, KD])
        modB = sb("modB", [P, 2, 2, KD])
        stat = sb("stat", [P, 72])

        ARENA = 19146
        arena = sb("arena", [P, ARENA])
        at = [0]

        def carve(words):
            v = arena[:, at[0]:at[0] + words]
            at[0] += words
            assert at[0] <= ARENA, at[0]
            return v

        qkT = carve(7 * TOK).rearrange("p (c n) -> p c n", c=7)
        vA = carve(NT * P).rearrange("p (t n) -> p t n", t=NT)
        vD = carve(NT * 2 * P).rearrange("p (t n) -> p t n", t=NT)
        stage = carve(2 * 896).rearrange("p (b n) -> p b n", b=2)
        soft = carve(3200)
        Pm = soft[:, 0:1920].rearrange("p (b n) -> p b n", b=3)
        PT = soft[:, 1920:3200].rearrange("p (b n) -> p b n", b=2)
        ra1, ra2, rd1, rd2 = soft[:, 0:384], soft[:, 384:768], soft[:, 768:1280], soft[:, 1280:1792]
        qsq = soft[:, 1792:2176]
        osq = stage[:, 1, 0:256]
        o_tok = carve(512)
        o_raw = carve(512)
        junk = o_tok.bitcast(BF16)
        poolT = carve(2 * SEQW).rearrange("p (i n) -> p i n", i=2)
        u = carve(2 * SEQW).rearrange("p (i n) -> p i n", i=2)
        y = carve(2 * OUTW)
        y3 = y.rearrange("p (i n) -> p i n", i=2)
        wa = carve(SEQW)
        wb = carve(SEQW)
        poolD = carve(2 * OUTW)
        poolD3 = poolD.rearrange("p (i n) -> p i n", i=2)
        sig, tap = wa[:, 0:TOK], wa[:, 0:OUTW]
        ysq = poolT.rearrange("p i n -> p (i n)")[:, 0:2 * OUTW].rearrange("p (i n) -> p i n", i=2)
        rstd_y = wb[:, 0:OUTW]
        xt = [poolD[:, 0:D], y[:, 0:D]]
        modrow = arena[0:2, 0:6 * D]
        at[0] = 0
        gb1 = carve(2 * D).rearrange("p (v n) -> p v n", v=2)
        xo = carve(2 * D).rearrange("p (b n) -> p b n", b=2)
        xnb = carve(2 * D).rearrange("p (b n) -> p b n", b=2)
        gated = carve(D)
        junk2 = carve(D // 2).bitcast(BF16)
        logit = carve(80)
        aff = carve(80)
        affT = carve(TOK)
        topv = carve(80)
        topi = carve(80).bitcast(U32)
        topf = carve(80)
        gateT = carve(17)
        idxT = carve(17).bitcast(U32)
        idxc = carve(2).bitcast(U32)
        gatec = carve(1)
        g2b = carve(D)
        xg = carve(2 * D).rearrange("p (b n) -> p b n", b=2)
        xeT = carve(KD * CAP).rearrange("p (j n) -> p j n", j=KD)
        sil = carve(D)
        hid = carve(D)
        hidT = carve(KD * CAP).rearrange("p (j n) -> p j n", j=KD)
        yb = carve(D)
        fgb = gb1[:, 0, :]

        PS = ctx.enter_context(nc.psum_tensor("PS", [P, 8, 512], F32))
        flat = PS[:, :, :].rearrange("p b n -> p (b n)")

        def pair(b, n=D):
            return flat[:, b * 512:b * 512 + n]

        x_dram = nc.dram_tensor("x_rows", [TOK, D], F32, kind="Internal").ap()
        xn_dram = nc.dram_tensor("xn_rows", [TOK, D], F32, kind="Internal").ap()
        modg = nc.dram_tensor("mod_gates", [2, 2, D], F32, kind="Internal").ap()

        const_loaded, x_seeded = sem("const_loaded"), sem("x_seeded")
        params_loaded = sem("params_loaded")
        slot_ready = [sem(f"slot_ready{s}") for s in range(6)]
        slot_used = [sem(f"slot_used{s}") for s in range(6)]
        phase_done = sem("phase_done")
        c_turned, silu_c = sem("c_turned"), sem("silu_c")
        tensor_chain = sem("vector_chain")
        pool_chain = sem("pool_chain")
        consts_set = sem("consts_set")
        waits_passed = sem("waits_passed")
        mod_evac, mod_turned = sem("mod_evac"), sem("mod_turned")
        kc_turned = sem("kc_turned")
        gates_saved = sem("gates_saved")
        lam_sums, lam_exps = sem("lam_sums"), sem("lam_exps")
        x_loaded = [sem("x_loaded0"), sem("x_loaded1")]
        n_ss, n_rstd, n_xn, n_xT = sem("n_ss"), sem("n_rstd"), sem("n_xn"), sem("n_xT")
        b0_evac, b1_evac = sem("b0_evac"), sem("b1_evac")
        p_mm, p_sq, p_ds, p_v, p_qs = sem("p_mm"), sem("p_sq"), sem("p_ds"), sem("p_v"), sem("p_qs")
        p_ms, p_r = sem("p_ms"), sem("p_r")
        ra_done, rd_done, q_T = sem("ra_done"), sem("rd_done"), sem("q_T")
        f_mm, f_act, f_u = sem("f_mm"), sem("f_act"), sem("f_u")
        pads_zero = sem("pads_zero")
        state_saved = sem("state_saved")
        t_scores, t_max, t_exp = sem("t_scores"), sem("t_max"), sem("t_exp")
        t_comb, t_pT, t_pt, t_pv = sem("t_comb"), sem("t_pT"), sem("t_pt"), sem("t_pv")
        t_od, t_dss, t_dr, t_otok = sem("t_od"), sem("t_dss"), sem("t_dr"), sem("t_otok")
        t_oT, t_oTe = sem("t_oT"), sem("t_oTe")
        c_mix, c_mean, c_yc, c_sq, c_var = sem("c_mix"), sem("c_mean"), sem("c_yc"), sem("c_sq"), sem("c_var")
        c_vs, c_rs, c_yn, c_z, c_pw, c_mixe = (sem("c_vs"), sem("c_rs"), sem("c_yn"), sem("c_z"), sem("c_pw"),
                                               sem("c_mixe"))
        g_loaded = sem("g_loaded")
        xo_loaded = [sem("xo_loaded0"), sem("xo_loaded1")]
        x_saved = [sem("x_saved0"), sem("x_saved1")]
        o_mm, o_g, o_x, o_ss, o_r, o_xn = sem("o_mm"), sem("o_g"), sem("o_x"), sem("o_ss"), sem("o_r"), sem("o_xn")
        o_xT, o_h4, o_h5, o_lg = sem("o_xT"), sem("o_h4"), sem("o_h5"), sem("o_lg")
        r_sub, r_exp, r_aff, r_affT, r_affs = (sem("r_sub"), sem("r_exp"), sem("r_aff"), sem("r_affT"),
                                               sem("r_affs"))
        k_top, k_T = sem("k_top"), sem("k_T")
        e_idx = sem("e_idx")
        e_gath = [sem("e_gath0"), sem("e_gath1")]
        e_X0, e_X1, e_xe = sem("e_X0"), sem("e_X1"), sem("e_xe")
        e_sil, e_U0, e_hid = sem("e_sil"), sem("e_U0"), sem("e_hid")
        e_T0, e_T1, e_hT0, e_hT1 = sem("e_T0"), sem("e_T1"), sem("e_hT0"), sem("e_hT1")
        e_y, e_scat, rows_added = sem("e_y"), sem("e_scat"), sem("rows_added")
        fin_x = [sem("fin_x0"), sem("fin_x1")]
        fin_g, fin_ss, fin_r, fin_y = sem("fin_g"), sem("fin_ss"), sem("fin_r"), sem("fin_y")
        fin_saved = [sem("fin_saved0"), sem("fin_saved1")]

        CREDIT = 1

        block = ctx.enter_context(nc.Block())

        def wait_apart(eng, semaphore, value):
            eng.wait_ge(semaphore, value)
            eng.sem_inc(waits_passed, 1)

        N_PARAMS = 27
        N_CONST = 8
        X_LOADS = (3, 2)
        MAPS, UNITS = 12, 8
        STEPS = NT * UNITS

        def parity_count(l, t):
            return l * X_LOADS[t % 2] + t // 2 + 1

        def head(uu):
            t, r = divmod(uu, UNITS)
            return t, r < 4, r % 4, t * MAPS + (r if r < 4 else 4 + 2 * (r - 4))

        def maps_of(uu):
            t, gqa, h, n = head(uu)
            return [n] if gqa else [n, n + 1]

        def unit_of(n):
            t, r = divmod(n, MAPS)
            return t * UNITS + (r if r < 4 else 4 + (r - 4) // 2)

        @block.sync
        def _(sp):
            for dst, src in ((ident[:, :], ins["k_ident"]),
                             (rope_a[:, :, :, :], ins["k_rope_a"].rearrange("(t p) a n -> p t a n", p=P)),
                             (rope_d[:, :, :, :], ins["k_rope_d"].rearrange("(t p) a n -> p t a n", p=P)),
                             (edge[:, :, :, :], ins["k_edge"]),
                             (invw[:, :], ins["k_invw"]),
                             (crow[0:8, :], ins["c"].rearrange("a (j p) -> (a j) p", p=P)),
                             (crow[8:16, :], ins["c_ctx"].rearrange("(j p) -> j p", p=P)),
                             (neghalf[:, :], ins["k_neghalf"])):
                sp.dma_start(dst, src).then_inc(const_loaded, 16)

            def slot_load(l, rnd, s, src):
                sp.wait_ge(slot_used[s], l * ROUNDS + rnd + CREDIT)
                sp.dma_start(ring[:, s, :, :], src.rearrange("(k p) n -> p k n", p=P)).then_inc(slot_ready[s], 16)

            with sp.Fori(0, LAYERS) as l:
                for rnd in range(2):
                    for m in range(3):
                        b = 3 * rnd + m
                        for h in range(2):
                            slot_load(l, rnd, 2 * m + h,
                                      ins["w_mod"][l, h * 512:(h + 1) * 512, b * D:(b + 1) * D])
                for m in range(2):
                    for h in range(2):
                        slot_load(l, 2, 2 * m + h, ins["w_in"][l, h * 512:(h + 1) * 512, m * D:(m + 1) * D])
                for h in range(2):
                    slot_load(l, 2, 4 + h, ins["w_out"][l, h * 512:(h + 1) * 512, :])
                with sp.Fori(0, EXPERTS) as e:
                    for m, w in enumerate(("exp_w_gate", "exp_w_up", "exp_w_down")):
                        for h in range(2):
                            slot_load(l, 3 + e, 2 * m + h, ins[w][l, e, h * 512:(h + 1) * 512, :])

        @block.tensor
        def _(pe):
            mm, tr = nc.tensor.matmul, nc.tensor.transpose
            for s in slot_used:
                pe.sem_inc(s, CREDIT)

            def finish_phase(l, k):
                pe.drain().then_inc(phase_done, 1)
                pe.wait_ge(phase_done, 4 * (l * PHASES + k))

            pe.wait_ge(const_loaded, 16 * N_CONST)
            tr(PS[:, 7, 0:16], crow[:, :], ident[0:16, 0:16]).then_inc(c_turned, 1)
            pe.wait_ge(silu_c, 1)
            pe.wait_ge(consts_set, 2)

            with pe.Fori(0, LAYERS) as l:
                for b in range(6):
                    rnd, m = divmod(b, 3)
                    if b >= 2:
                        pe.wait_ge(mod_evac, 6 * l + b - 1)
                    for h in range(2):
                        pe.wait_ge(slot_ready[2 * m + h], 16 * (l * ROUNDS + rnd + 1))
                        for kk in range(4):
                            k = 4 * h + kk
                            for c in range(2):
                                last = mm(PS[0:2, 2 * (b % 2) + c, :], scT[:, :, k],
                                          ring[:, 2 * m + h, kk, c * 512:(c + 1) * 512],
                                          start=(k == 0), stop=(k == KD - 1))
                        last.then_inc(slot_used[2 * m + h], 1)
                pe.wait_ge(params_loaded, 16 * N_PARAMS * (l + 1))
                for i in range(3):
                    last = tr(PS[:, 7, i * P:(i + 1) * P], ck[:, i * P:(i + 1) * P], ident[:, :])
                last.then_inc(kc_turned, 1)
                tr(PS[:, 4, 64:88], prow[:, :], ident[0:24, 0:24])
                for i in range(2):
                    tr(PS[:, 4, 96 + 32 * i:96 + 32 * i + TAPS], cwrow[:, i * P:(i + 1) * P],
                       ident[0:TAPS, 0:TAPS])
                wait_apart(pe, mod_evac, 6 * l + 6)
                for bi, b in enumerate((0, 1, 3, 4)):
                    for j in range(KD):
                        c0 = 2 * (bi * KD + j)
                        last = tr(PS[:, 4, c0:c0 + 2], modrow[:, b * D + j * P:b * D + (j + 1) * P],
                                  ident[0:2, 0:2])
                last.then_inc(mod_turned, 1)
                finish_phase(l, 1)

                uses = [0]

                def banks01(l):
                    if uses[0]:
                        pe.wait_ge(b0_evac, 10 * l + uses[0])
                        pe.wait_ge(b1_evac, 10 * l + uses[0])
                    uses[0] += 1

                def step_x(l, t):
                    pe.wait_ge(n_xn, NT * l + t + 1)
                    banks01(l)
                    for j in range(KD):
                        last = tr(PS[:, j // 4, (j % 4) * P:(j % 4 + 1) * P], xt[t % 2][:, j * P:(j + 1) * P],
                                  ident[:, :])
                    last.then_inc(n_xT, 1)

                def step_j(l, t):
                    pe.wait_ge(b0_evac, 10 * l + XUSE[t] + 1)
                    pe.wait_ge(b1_evac, 10 * l + XUSE[t] + 1)
                    if t >= 2:
                        pe.wait_ge(p_v, NT * l + t - 1)
                        pe.wait_ge(p_qs, NT * l + t - 1)
                    b0 = 2 + 3 * (t % 2)
                    if t == 0:
                        for s in range(4):
                            pe.wait_ge(slot_ready[s], 16 * (l * ROUNDS + 3))
                    for k in range(KD):
                        s, kk = k // 4, k % 4
                        lhs = H[:, k, t * P:(t + 1) * P]
                        mm(PS[:, b0, :], lhs, ring[:, s, kk, 0:512], start=(k == 0), stop=(k == KD - 1))
                        mm(PS[:, b0 + 1, :], lhs, ring[:, 2 + s, kk, 256:768], start=(k == 0), stop=(k == KD - 1))
                        last = mm(PS[:, b0 + 2, 0:256], lhs, ring[:, 2 + s, kk, 768:1024],
                                  start=(k == 0), stop=(k == KD - 1))
                    last.then_inc(p_mm, 1)

                def step_q(l, t):
                    pe.wait_ge(ra_done, NT * l + t + 1)
                    if t < LT:
                        pe.wait_ge(rd_done, LT * l + t + 1)
                    else:
                        pe.wait_ge(p_ds, NT * l + t + 1)
                    banks01(l)
                    st = stage[:, t % 2, :]
                    for c in range(7):
                        last = tr(PS[:, c // 4, (c % 4) * P:(c % 4 + 1) * P], st[:, c * P:(c + 1) * P],
                                  ident[:, :])
                    last.then_inc(q_T, 1)

                def step_f(l, n):
                    if n == 0:
                        pe.wait_ge(p_v, NT * l + NT)
                        pe.wait_ge(p_qs, NT * l + NT)
                    if n >= 3:
                        pe.wait_ge(f_act, 4 * l + n - 2)
                    s0, c0 = FCHUNK[n]
                    for k in range(KD):
                        lhs = ring[:, s0 + k // 4, k % 4, c0:c0 + P]
                        mm(PS[:, 2 + 2 * (n % 3), :], lhs, H[:, k, 0:LAT], start=(k == 0), stop=(k == KD - 1))
                        last = mm(PS[:, 3 + 2 * (n % 3), 0:CTX], lhs, H[:, k, LAT:TOK],
                                  start=(k == 0), stop=(k == KD - 1))
                    last.then_inc(f_mm, 1)

                for kind, n in ORDER:
                    if kind == "x":
                        step_x(l, n)
                    elif kind == "j":
                        step_j(l, n)
                    elif kind == "q":
                        step_q(l, n)
                    elif kind == "f":
                        step_f(l, n)
                pe.wait_ge(f_mm, 6 * l + 6)
                for s in range(4):
                    pe.nop().then_inc(slot_used[s], 1)
                finish_phase(l, 2)

                def scores(l, n):
                    uu = unit_of(n)
                    t, gqa, h, n0 = head(uu)
                    if n >= 2:
                        pe.wait_ge(t_exp, NT * MAPS * l + n - 1)
                    b0 = 2 * (n % 2)
                    if gqa:
                        p0, kd, qc, kc = HD * (h // 2), HD, h % 2, 2
                        cc = 0
                    else:
                        p0, kd, qc, kc = HD * (h % 2) + 32 * (n - n0), 32, 3 + h // 2, 5 + h // 2
                        cc = 1 + h // 2
                    lhs = qkT[p0:p0 + kd, qc, t * P:(t + 1) * P]
                    if t < LT:
                        mm(PS[:, b0, :], lhs, qkT[p0:p0 + kd, kc, 0:LAT], start=True, stop=True)
                        last = mm(PS[:, b0 + 1, 0:P], lhs, kcT[p0:p0 + kd, cc, :], start=True, stop=True)
                    else:
                        last = mm(PS[:, b0, 0:P], lhs, qkT[p0:p0 + kd, kc, LAT:TOK], start=True, stop=True)
                    last.then_inc(t_scores, 1)

                def turn_probs(l, uu):
                    t, gqa, h, n0 = head(uu)
                    n = maps_of(uu)[-1]
                    if gqa:
                        pe.wait_ge(t_exp, NT * MAPS * l + n + 1)
                    else:
                        pe.wait_ge(t_comb, 4 * NT * l + 4 * t + h + 1)
                    if uu >= 1:
                        pe.wait_ge(t_pt, STEPS * l + uu)
                    for c in range(LT + 1 if t < LT else 1):
                        last = tr(PS[:, 4 + c // 4, (c % 4) * P:(c % 4 + 1) * P],
                                  Pm[:, n % 3, c * P:(c + 1) * P], ident[:, :])
                    last.then_inc(t_pT, 1)

                def values(l, uu):
                    t, gqa, h, n0 = head(uu)
                    if uu % UNITS == 0 and t >= 2:
                        pe.wait_ge(t_oTe, NT * l + t - 1)
                    pe.wait_ge(t_pt, STEPS * l + uu + 1)
                    n = LT + 1 if t < LT else 1
                    o0 = h * HD if gqa else 256 + h * HD
                    for c in range(n):
                        kt = c if t < LT else LT
                        if c == LT:
                            v = cv[:, HD * (h // 2):HD * (h // 2 + 1)] if gqa else cv[:, P + HD * h:P + HD * (h + 1)]
                        else:
                            v = vA[:, kt, HD * (h // 2):HD * (h // 2 + 1)] if gqa else vD[:, kt, HD * h:HD * (h + 1)]
                        last = mm(PS[:, 6 + t % 2, o0:o0 + HD], PT[:, uu % 2, c * P:(c + 1) * P], v,
                                  start=(c == 0), stop=(c == n - 1))
                    last.then_inc(t_pv, 1)

                def turn_out(l, t):
                    pe.wait_ge(t_otok, NT * l + t + 1)
                    for c in range(4):
                        last = tr(PS[:, 6 + t % 2, c * P:(c + 1) * P], o_tok[:, c * P:(c + 1) * P], ident[:, :])
                    last.then_inc(t_oT, 1)

                scores(l, 0)
                for uu in range(STEPS + 3):
                    if uu + 1 < STEPS:
                        for n in maps_of(uu + 1):
                            scores(l, n)
                    if uu < STEPS:
                        turn_probs(l, uu)
                    if 1 <= uu <= STEPS:
                        values(l, uu - 1)
                    if uu >= UNITS + 2 and (uu - 2) % UNITS == 0:
                        turn_out(l, (uu - 2) // UNITS - 1)
                finish_phase(l, 3)

                for i in range(2):
                    mm(PS[:, 2 * i, :], pool_w[:, i, :], poolD3[:, i, 0:LAT], start=True, stop=True)
                    mm(PS[:, 2 * i + 1, 0:CTX], pool_w[:, i, :], poolD3[:, i, CTX0 - PAD:OUTW],
                       start=True, stop=True).then_inc(c_mix, 1)

                def channel_mean(b, src, done):
                    for i in range(2):
                        mm(PS[:, b, :], mean_w[:, :], src[:, i, 0:512], start=(i == 0), stop=(i == 1))
                        last = mm(PS[:, b + 1, 0:OUTW - 512], mean_w[:, :], src[:, i, 512:OUTW],
                                  start=(i == 0), stop=(i == 1))
                    last.then_inc(done, 1)

                channel_mean(4, y3, c_mean)
                pe.wait_ge(c_sq, 2 * l + 2)
                channel_mean(6, ysq, c_var)
                pe.wait_ge(c_z, 2 * l + 2)
                pe.wait_ge(c_mixe, 4 * l + 2)
                for co in range(2):
                    for ci in range(2):
                        lhs = conv_pw[:, ci, co * P:(co + 1) * P]
                        mm(PS[:, 2 * co, :], lhs, y3[:, ci, 0:LAT], start=(ci == 0), stop=(ci == 1))
                        last = mm(PS[:, 2 * co + 1, 0:CTX], lhs, y3[:, ci, CTX0 - PAD:OUTW],
                                  start=(ci == 0), stop=(ci == 1))
                    last.then_inc(c_pw, 1)
                finish_phase(l, 4)

                def project_out(l, t):
                    if t >= 2:
                        pe.wait_ge(o_g, NT * l + t - 1)
                    if t == 0:
                        for s in (4, 5):
                            pe.wait_ge(slot_ready[s], 16 * (l * ROUNDS + 3))
                    for k in range(KD):
                        for c in range(2):
                            last = mm(PS[:, 2 * (t % 2) + c, :], H[:, k, t * P:(t + 1) * P],
                                      ring[:, 4 + k // 4, k % 4, c * 512:(c + 1) * 512],
                                      start=(k == 0), stop=(k == KD - 1))
                    last.then_inc(o_mm, 1)

                def norm2_turn(l, t):
                    pe.wait_ge(o_xn, NT * l + t + 1)
                    if t >= 1:
                        pe.wait_ge(o_h4, NT * l + t)
                        pe.wait_ge(o_h5, NT * l + t)
                    for j in range(KD):
                        last = tr(PS[:, 4 + j // 4, (j % 4) * P:(j % 4 + 1) * P],
                                  xnb[:, t % 2, j * P:(j + 1) * P], ident[:, :])
                    last.then_inc(o_xT, 1)

                def route(l, t):
                    pe.wait_ge(o_h4, NT * l + t + 1)
                    pe.wait_ge(o_h5, NT * l + t + 1)
                    for k in range(KD):
                        last = mm(PS[:, 6, t * EXPERTS:(t + 1) * EXPERTS], H[:, k, t * P:(t + 1) * P],
                                  router[:, k, :], start=(k == 0), stop=(k == KD - 1))
                    last.then_inc(o_lg, 1)

                project_out(l, 0)
                for t in range(NT):
                    if t + 1 < NT:
                        project_out(l, t + 1)
                    norm2_turn(l, t)
                    route(l, t)
                pe.wait_ge(o_mm, NT * l + NT)
                for s in (4, 5):
                    pe.nop().then_inc(slot_used[s], 1)
                pe.wait_ge(r_aff, l + 1)
                for t in range(NT):
                    dst = PS[0:EXPERTS, 7, t * P:(t + 1) * P] if t < LT else PS[0:EXPERTS, 6, P:2 * P]
                    last = tr(dst, aff[:, t * EXPERTS:(t + 1) * EXPERTS], ident[:, :])
                last.then_inc(r_affT, 1)
                wait_apart(pe, k_top, l + 1)
                tr(PS[0:CAP, 0, 0:EXPERTS], topf[0:EXPERTS, :], ident[0:EXPERTS, 0:EXPERTS])
                tr(PS[0:CAP, 0, 16:16 + EXPERTS], topv[0:EXPERTS, :],
                   ident[0:EXPERTS, 0:EXPERTS]).then_inc(k_T, 1)
                finish_phase(l, 5)

                def turn_rows(part, xp, done):
                    for j in range(4):
                        jj = 4 * part + j
                        last = tr(PS[:, 6 + part, j * CAP:(j + 1) * CAP], xg[0:CAP, xp, jj * P:(jj + 1) * P],
                                  ident[0:CAP, 0:CAP])
                    last.then_inc(done, 1)

                def expert(l, e, e2, p):
                    done = l * EXPERTS + e
                    rnd = l * ROUNDS + 3 + e
                    pe.wait_ge(e_xe, 17 * l + e + 1)
                    pe.wait_ge(e_sil, 2 * done + CREDIT)
                    for h in range(2):
                        pe.wait_ge(slot_ready[h], 16 * (rnd + 1))
                        for kk in range(4):
                            k = 4 * h + kk
                            for c in range(2):
                                last = mm(PS[0:CAP, c, :], xeT[:, k, :], ring[:, h, kk, c * 512:(c + 1) * 512],
                                          start=(k == 0), stop=(k == KD - 1))
                        last.then_inc(slot_used[h], 1)
                    pe.wait_ge(e_hid, 2 * done + CREDIT)
                    for h in range(2):
                        pe.wait_ge(slot_ready[2 + h], 16 * (rnd + 1))
                    for c in range(2):
                        for k in range(KD):
                            last = mm(PS[0:CAP, 2 + c, :], xeT[:, k, :],
                                      ring[:, 2 + k // 4, k % 4, c * 512:(c + 1) * 512],
                                      start=(k == 0), stop=(k == KD - 1))
                            if c == 1 and k % 4 == 3:
                                last.then_inc(slot_used[2 + k // 4], 1)
                        if c == 0:
                            last.then_inc(e_U0, 1)

                    def turn_hidden(part, done_sem):
                        pe.wait_ge(e_hid, 2 * done + 1 + part + CREDIT)
                        for j in range(4):
                            jj = 4 * part + j
                            last = tr(PS[:, 6 + part, j * CAP:(j + 1) * CAP], hid[0:CAP, jj * P:(jj + 1) * P],
                                      ident[0:CAP, 0:CAP])
                        last.then_inc(done_sem, 1)

                    def down(k):
                        for c in range(2):
                            last = mm(PS[0:CAP, 4 + c, :], hidT[:, k, :],
                                      ring[:, 4 + k // 4, k % 4, c * 512:(c + 1) * 512],
                                      start=(k == 0), stop=(k == KD - 1))
                        if k % 4 == 3:
                            last.then_inc(slot_used[4 + k // 4], 1)

                    turn_hidden(0, e_T0)
                    pe.wait_ge(e_hT0, done + 1)
                    pe.wait_ge(e_y, done + CREDIT)
                    pe.wait_ge(slot_ready[4], 16 * (rnd + 1))
                    for k in range(3):
                        down(k)
                    turn_hidden(1, e_T1)
                    down(3)
                    pe.wait_ge(e_gath[1 - p], 16 * (l * (8 + p) + e2 + 1))
                    turn_rows(0, 1 - p, e_X0)
                    pe.wait_ge(e_hT1, done + 1)
                    pe.wait_ge(slot_ready[5], 16 * (rnd + 1))
                    down(4)
                    down(5)
                    turn_rows(1, 1 - p, e_X1)
                    down(6)
                    down(7)

                pe.wait_ge(e_gath[0], 16 * (9 * l + 1))
                turn_rows(0, 0, e_X0)
                turn_rows(1, 0, e_X1)
                with pe.Fori(0, EXPERTS // 2) as e2:
                    expert(l, 2 * e2, e2, 0)
                    expert(l, 2 * e2 + 1, e2 + 1, 1)
                finish_phase(l, 6)

        @block.scalar
        def _(act):
            do = nc.scalar.activation
            act.sem_inc(e_sil, CREDIT)

            def finish_phase(l, k):
                act.drain().then_inc(phase_done, 1)
                act.wait_ge(phase_done, 4 * (l * PHASES + k))

            act.dma_start(x_dram[0:LAT, :], ins["x_sample"][0, :, :]).then_inc(x_seeded, 16)
            act.dma_start(x_dram[LAT:TOK, :], ins["x_prompt"][0, :, :]).then_inc(x_seeded, 16)
            act.wait_ge(c_turned, 1)
            do(scT[:, :, :].rearrange("p v j -> p (v j)"), PS[:, 7, 0:16], ACT.Silu).then_inc(silu_c, 1)
            act.wait_ge(x_seeded, 32)
            act.wait_ge(consts_set, 2)

            with act.Fori(0, LAYERS) as l:
                def load(dst, src):
                    act.dma_start(dst, src).then_inc(params_loaded, 16)

                for v in range(2):
                    load(modrow[v:v + 1, :], ins["b_mod"][bass.ds(l, 1), :])
                for r0, name, n in ((0, "norm1_g", 8), (8, "norm2_g", 8), (16, "pool_scale", 2),
                                    (18, "conv_dw_b", 2), (20, "conv_ln_g", 2), (22, "conv_ln_b", 2)):
                    load(prow[r0:r0 + n, :], ins[name][l, :].rearrange("(j p) -> j p", p=P))
                load(cwrow[:, :], ins["conv_dw_w"][l, :, :])
                for i, name in enumerate(("gqa_qn_g", "gqa_kn_g", "diff_subln_g")):
                    load(head_g[:, i, :], ins[name][bass.ds(l, 1), :].to_broadcast([P, HD]))
                for i, name in enumerate(("diff_lq1", "diff_lk1", "diff_lq2", "diff_lk2")):
                    load(lamv[:, i, :], ins[name][bass.ds(l, 1), :].to_broadcast([P, 32]))
                load(lamc[:, :], ins["k_lam"][bass.ds(l, 1), :].to_broadcast([P, 2]))
                load(router[:, :, :], ins["router_w"][l, :, :].rearrange("(k p) e -> p k e", p=P))
                for g in range(4):
                    r0 = HD * (g % 2)
                    load(pool_w[r0:r0 + HD, g // 2, r0:r0 + HD], ins["pool_w"][l, g, :, :])
                load(conv_pw[:, :, :], ins["conv_pw_w"][l, :, :].rearrange("(i p) n -> p i n", p=P))
                load(ck[:, 0:P], ins["cache_gqa_k"][0, l, :, :, :].rearrange("t h d -> t (h d)"))
                load(ck[:, P:384], ins["cache_diff_k"][0, l, :, :, :].rearrange("t h d -> t (h d)"))
                load(cv[:, 0:P], ins["cache_gqa_v"][0, l, :, :, :].rearrange("t h d -> t (h d)"))
                load(cv[:, P:384], ins["cache_diff_v"][0, l, :, :, :].rearrange("t h d -> t (h d)"))
                act.wait_ge(lam_sums, l + 1)
                do(lams[:, 2:4], lams[:, 0:2], ACT.Exp).then_inc(lam_exps, 1)
                act.wait_ge(kc_turned, l + 1)
                do(kcT[:, :, :].rearrange("p i n -> p (i n)"), PS[:, 7, 0:384], ACT.Copy)
                act.wait_ge(mod_evac, 6 * l + 6)
                for i, b in enumerate((2, 5)):
                    act.dma_start(modg[:, i, :], modrow[:, b * D:(b + 1) * D]).then_inc(gates_saved, 16)
                wait_apart(act, gates_saved, 32 * (l + 1))
                finish_phase(l, 1)

                def load_x(l, t):
                    if t >= 2:
                        act.wait_ge(n_xT, NT * l + t - 1)
                    act.dma_start(xt[t % 2], x_dram[t * P:(t + 1) * P, :]).then_inc(x_loaded[t % 2], 16)

                def squares(l, t):
                    act.wait_ge(x_loaded[t % 2], 16 * parity_count(l, t))
                    if t >= 1:
                        act.wait_ge(n_ss, NT * l + t)
                    do(junk, xt[t % 2], ACT.Square, accum_out=stat[:, t:t + 1]).then_inc(n_ss, 1)

                def step_x(l, t):
                    act.wait_ge(n_xT, NT * l + t + 1)
                    v = 0 if t < LT else 1
                    for j in range(4):
                        last = do(H[:, j, t * P:(t + 1) * P], PS[:, 0, j * P:(j + 1) * P], ACT.Identity,
                                  bias=modB[:, 0, v, j:j + 1], scale=modA[:, 0, v, j:j + 1])
                    last.then_inc(b0_evac, 1)

                def step_j(l, t):
                    b0 = 2 + 3 * (t % 2)
                    act.wait_ge(p_mm, NT * l + t + 1)
                    if t >= 1:
                        act.wait_ge(p_ms, NT * l + t)
                    do(vA[:, t, :], PS[:, b0, 384:512], ACT.Copy)
                    do(qsq, PS[:, b0, 0:384], ACT.Square).then_inc(p_sq, 1)
                    if t >= 2:
                        act.wait_ge(q_T, NT * l + t - 1)
                    do(stage[:, t % 2, 384:896], PS[:, b0 + 1, :], ACT.Copy).then_inc(p_ds, 1)
                    do(vD[:, t, :], PS[:, b0 + 2, 0:256], ACT.Copy).then_inc(p_v, 1)

                def step_q(l, t):
                    act.wait_ge(q_T, NT * l + t + 1)
                    do(qkT[:, 0:4, t * P:(t + 1) * P], PS[:, 0, :].rearrange("p (c n) -> p c n", c=4),
                       ACT.Copy).then_inc(b0_evac, 1)

                def step_f(l, n):
                    if n in (3, 5):
                        return
                    src = pair(2 + 2 * (n % 3), TOK)
                    act.wait_ge(f_mm, 6 * l + n + 1)
                    if n < 2:
                        do(poolT[:, n, PAD:PAD + LAT], src[:, 0:LAT], ACT.Copy)
                        do(poolT[:, n, CTX0:CTX0 + CTX], src[:, LAT:TOK], ACT.Copy).then_inc(f_act, 1)
                    else:
                        if n == 4:
                            act.wait_ge(f_u, 2 * l + 1)
                        do(sig, src, ACT.Sigmoid).then_inc(f_act, 1)

                load_x(l, 0)
                load_x(l, 1)
                squares(l, 0)
                squares(l, 1)
                for kind, n in ORDER:
                    if kind == "x":
                        step_x(l, n)
                        if n + 2 < NT:
                            load_x(l, n + 2)
                    elif kind == "s":
                        squares(l, n)
                    elif kind == "j":
                        step_j(l, n)
                    elif kind == "q":
                        step_q(l, n)
                    elif kind == "f":
                        step_f(l, n)
                act.wait_ge(p_v, NT * l + NT)
                act.wait_ge(ra_done, NT * l + NT)
                for name, src in (("state_gqa_k", stage[:, 0, 256:384]), ("state_gqa_v", vA[:, LT, :]),
                                  ("state_diff_k", stage[:, 0, 640:896]), ("state_diff_v", vD[:, LT, :])):
                    act.dma_start(outs[name][0, l, :, :, :].rearrange("t h d -> t (h d)"), src)\
                       .then_inc(state_saved, 16)
                finish_phase(l, 2)

                def exponentials(l, n):
                    uu = unit_of(n)
                    t, gqa, h, n0 = head(uu)
                    act.wait_ge(t_max, NT * MAPS * l + n + 1)
                    if n >= 3:
                        act.wait_ge(t_pT, STEPS * l + unit_of(n - 3) + 1)
                    w = TOK if t < LT else P
                    do(Pm[:, n % 3, 0:w], pair(2 * (n % 2), w), ACT.Exp, bias=stat[:, 8 + n % 4:9 + n % 4],
                       scale=(HD ** -0.5 if gqa else 32 ** -0.5),
                       accum_out=stat[:, 12 + n % 4:13 + n % 4]).then_inc(t_exp, 1)

                def take_probs(l, uu):
                    t, gqa, h, n0 = head(uu)
                    act.wait_ge(t_pT, STEPS * l + uu + 1)
                    if uu >= 2:
                        act.wait_ge(t_pv, STEPS * l + uu - 1)
                    w = TOK if t < LT else P
                    do(PT[:, uu % 2, 0:w], pair(4, w), ACT.Copy).then_inc(t_pt, 1)

                def take_heads(l, t):
                    act.wait_ge(t_pv, STEPS * l + UNITS * (t + 1))
                    if t >= 1:
                        act.wait_ge(t_otok, NT * l + t)
                    do(o_raw, PS[:, 6 + t % 2, :], ACT.Copy).then_inc(t_od, 1)

                def take_out(l, t):
                    act.wait_ge(t_oT, NT * l + t + 1)
                    src = PS[:, 6 + t % 2, :].rearrange("p (c n) -> p c n", c=4)
                    do(H[:, 0:2, t * P:(t + 1) * P], src[:, 0:2, :], ACT.Copy)
                    do(H[:, 6:8, t * P:(t + 1) * P], src[:, 2:4, :], ACT.Copy).then_inc(t_oTe, 1)

                exponentials(l, 0)
                for uu in range(STEPS + 3):
                    if uu < STEPS and len(maps_of(uu)) == 1:
                        take_probs(l, uu)
                    if uu + 1 < STEPS:
                        for n in maps_of(uu + 1):
                            exponentials(l, n)
                    if uu < STEPS and len(maps_of(uu)) == 2:
                        take_probs(l, uu)
                    if uu >= UNITS and uu % UNITS == 0:
                        take_heads(l, uu // UNITS - 1)
                    if uu >= UNITS + 2 and (uu - 2) % UNITS == 0:
                        take_out(l, (uu - 2) // UNITS - 1)
                wait_apart(act, state_saved, 64 * (l + 1))
                finish_phase(l, 3)

                def take_mix(i, src, chunk, done, scale=1.0):
                    do(H[:, chunk, :], src, ACT.Copy, scale=scale).then_inc(done, 1)

                for i in range(2):
                    act.wait_ge(c_mix, 2 * l + i + 1)
                    take_mix(i, pair(2 * i, TOK), 2 + i, c_mixe, scale=pT[:, 16 + i:17 + i])
                for i in range(2):
                    act.wait_ge(c_yc, 2 * l + i + 1)
                    do(ysq[:, i, :], y3[:, i, :], ACT.Square).then_inc(c_sq, 1)
                for i in range(2):
                    act.wait_ge(c_yn, 2 * l + i + 1)
                    do(y3[:, i, :], y3[:, i, :], ACT.Silu, bias=pT[:, 22 + i:23 + i],
                       scale=pT[:, 20 + i:21 + i]).then_inc(c_z, 1)
                for i in range(2):
                    act.wait_ge(c_pw, 2 * l + i + 1)
                    take_mix(i, pair(2 * i, TOK), 4 + i, c_mixe)
                finish_phase(l, 4)

                for v in range(2):
                    act.dma_start(gb1[:, v, :], modg[v:v + 1, 0, :].to_broadcast([P, D])).then_inc(g_loaded, 16)
                act.dma_start(g2b[0:CAPL, :], modg[0:1, 1, :].to_broadcast([CAPL, D])).then_inc(g_loaded, 16)
                act.dma_start(g2b[CAPL:CAP, :], modg[1:2, 1, :].to_broadcast([CAPC, D])).then_inc(g_loaded, 16)

                def load_xo(l, t):
                    if t >= 2:
                        act.wait_ge(x_saved[t % 2], 32 * parity_count(l, t - 2))
                    act.dma_start(xo[:, t % 2, :], x_dram[t * P:(t + 1) * P, :]).then_inc(xo_loaded[t % 2], 16)

                load_xo(l, 0)
                load_xo(l, 1)
                for t in range(NT):
                    act.wait_ge(o_x, NT * l + t + 1)
                    if t >= 1:
                        act.wait_ge(o_ss, NT * l + t)
                    do(junk2, xo[:, t % 2, :], ACT.Square, accum_out=stat[:, 16 + t:17 + t]).then_inc(o_ss, 1)
                    act.dma_start(x_dram[t * P:(t + 1) * P, :], xo[:, t % 2, :]).then_inc(x_saved[t % 2], 16)
                    act.wait_ge(o_xn, NT * l + t + 1)
                    act.dma_start(xn_dram[t * P:(t + 1) * P, :], xnb[:, t % 2, :]).then_inc(x_saved[t % 2], 16)
                    act.wait_ge(o_xT, NT * l + t + 1)
                    v = 0 if t < LT else 1
                    for j in range(4):
                        last = do(H[:, j, t * P:(t + 1) * P], PS[:, 4, j * P:(j + 1) * P], ACT.Identity,
                                  bias=modB[:, 1, v, j:j + 1], scale=modA[:, 1, v, j:j + 1])
                    last.then_inc(o_h4, 1)
                    if t + 2 < NT:
                        load_xo(l, t + 2)
                act.wait_ge(r_sub, l + 1)
                do(logit, logit, ACT.Exp).then_inc(r_exp, 1)
                act.wait_ge(r_affT, l + 1)
                do(affT[0:EXPERTS, 0:LAT], PS[0:EXPERTS, 7, :], ACT.Copy)
                do(affT[0:EXPERTS, LAT:TOK], PS[0:EXPERTS, 6, P:2 * P], ACT.Copy).then_inc(r_affs, 1)
                for p in range(2):
                    wait_apart(act, x_saved[p], 32 * X_LOADS[p] * (l + 1))
                finish_phase(l, 5)

                def take_rows(l, n):
                    for part, turned in ((0, e_X0), (1, e_X1)):
                        act.wait_ge(turned, 17 * l + n + 1)
                        for j in range(4):
                            jj = 4 * part + j
                            for v, c0, c1 in ((0, 0, CAPL), (1, CAPL, CAP)):
                                last = do(xeT[:, jj, c0:c1], PS[:, 6 + part, j * CAP + c0:j * CAP + c1],
                                          ACT.Identity, bias=modB[:, 1, v, jj:jj + 1],
                                          scale=modA[:, 1, v, jj:jj + 1])
                    last.then_inc(e_xe, 1)

                take_rows(l, 0)
                with act.Fori(0, EXPERTS) as e:
                    done = l * EXPERTS + e
                    act.wait_ge(slot_used[1], l * ROUNDS + 4 + e + CREDIT)
                    act.wait_ge(e_hid, 2 * done + CREDIT)
                    for c in range(2):
                        do(sil[0:CAP, c * 512:(c + 1) * 512], PS[0:CAP, c, :], ACT.Silu).then_inc(e_sil, 1)
                    take_rows(l, e + 1)
                finish_phase(l, 6)

            act.dma_start(fgb, ins["final_g"].rearrange("(a n) -> a n", a=1).to_broadcast([P, D])).then_inc(fin_g, 16)

            def fin_load(t):
                if t >= 2:
                    act.wait_ge(fin_saved[t % 2], 16 * (t // 2))
                act.dma_start(xo[:, t % 2, :], x_dram[t * P:(t + 1) * P, :]).then_inc(fin_x[t % 2], 16)

            fin_load(0)
            fin_load(1)
            for t in range(NT):
                act.wait_ge(fin_x[t % 2], 16 * (t // 2 + 1))
                if t >= 1:
                    act.wait_ge(fin_ss, t)
                do(junk2, xo[:, t % 2, :], ACT.Square, accum_out=stat[:, 16 + t:17 + t]).then_inc(fin_ss, 1)
                act.wait_ge(fin_y, t + 1)
                dst = outs["y_sample"][0, t * P:(t + 1) * P, :] if t < LT else outs["y_prompt"][0, :, :]
                act.dma_start(dst, xo[:, t % 2, :]).then_inc(fin_saved[t % 2], 16)
                if t + 2 < NT:
                    fin_load(t + 2)
            for p in range(2):
                act.wait_ge(fin_saved[p], 16 * X_LOADS[p])

        @block.vector
        def _(dve):
            V = nc.vector
            dve.sem_inc(e_hid, CREDIT)
            dve.sem_inc(e_y, CREDIT)
            chain = [0, 0]

            def link(ins_, bare=False):
                chain[0] += 1
                ins_.then_inc(tensor_chain, 1)
                if bare:
                    wait_apart(dve, tensor_chain, chain[1] + chain[0])
                else:
                    dve.wait_ge(tensor_chain, chain[1] + chain[0])

            def finish_phase(l, k):
                dve.drain().then_inc(phase_done, 1)
                dve.wait_ge(phase_done, 4 * (l * PHASES + k))

            def heads(ap, n):
                return ap.rearrange("p (h d) -> p h d", h=n)

            with dve.Fori(0, LAYERS) as l:
                chain[0], chain[1] = 0, l * V_LINKS
                dve.wait_ge(params_loaded, 16 * N_PARAMS * (l + 1))
                link(V.tensor_tensor(lamw[:, :, :], lamv[:, 0:4:2, :], lamv[:, 1:4:2, :], ALU.mult))
                V.tensor_reduce(lams[:, 0:2], lamw[:, :, :], AX.X, ALU.add).then_inc(lam_sums, 1)
                V.tensor_scalar(subg[:, :], head_g[:, 2, :], lamc[:, 1:2], None, ALU.mult)
                dve.wait_ge(lam_exps, l + 1)
                link(V.tensor_tensor(lams[:, 4:5], lams[:, 3:4], lams[:, 2:3], ALU.subtract))
                V.tensor_scalar(lams[:, 5:6], lams[:, 4:5], lamc[:, 0:1], None, ALU.subtract)
                for b in range(6):
                    rnd, m = divmod(b, 3)
                    dve.wait_ge(slot_used[2 * m + 1], l * ROUNDS + rnd + 1 + CREDIT)
                    V.tensor_tensor(modrow[:, b * D:(b + 1) * D], pair(2 * (b % 2))[0:2, :],
                                    modrow[:, b * D:(b + 1) * D], ALU.add).then_inc(mod_evac, 1)
                dve.wait_ge(mod_turned, l + 1)
                V.tensor_copy(cwT[:, :, 0:TAPS],
                              PS[:, 4, 96:160].rearrange("p (i n) -> p i n", i=2)[:, :, 0:TAPS])
                link(V.tensor_copy(pT[:, :], PS[:, 4, 64:88]))
                modT = PS[:, 4, 0:64].rearrange("p (b j v) -> p b v j", b=4, j=KD)
                for n in range(2):
                    V.tensor_copy(modB[:, n, :, :], modT[:, 2 * n, :, :])
                    for v in range(2):
                        V.scalar_tensor_tensor(modA[:, n, v, :], modT[:, 2 * n + 1, v, :], 1.0,
                                               pT[:, KD * n:KD * (n + 1)], ALU.add, ALU.mult)
                finish_phase(l, 1)

                def normalise(l, t):
                    dve.wait_ge(n_rstd, NT * l + t + 1)
                    V.tensor_scalar(xt[t % 2], xt[t % 2], stat[:, 24 + t:25 + t], None, ALU.mult).then_inc(n_xn, 1)

                def step_x(l, t):
                    dve.wait_ge(n_xT, NT * l + t + 1)
                    v = 0 if t < LT else 1
                    for j in range(4):
                        last = V.tensor_scalar(H[:, 4 + j, t * P:(t + 1) * P], PS[:, 1, j * P:(j + 1) * P],
                                               modA[:, 0, v, 4 + j:5 + j], modB[:, 0, v, 4 + j:5 + j],
                                               ALU.mult, ALU.add)
                    last.then_inc(b1_evac, 1)

                def step_j(l, t):
                    b0 = 2 + 3 * (t % 2)
                    st = stage[:, t % 2, 0:384]
                    dve.wait_ge(p_sq, NT * l + t + 1)
                    V.tensor_reduce(stat[:, 32:38], heads(qsq, 6), AX.X, ALU.add).then_inc(p_ms, 1)
                    dve.wait_ge(p_r, NT * l + t + 1)
                    if t >= 2:
                        dve.wait_ge(q_T, NT * l + t - 1)
                    V.tensor_tensor(st[:, 0:256].rearrange("p (c g d) -> p g c d", c=2, g=2),
                                    PS[:, b0, 0:256].rearrange("p (g c d) -> p g c d", c=2, g=2),
                                    stat[:, 38:42].rearrange("p (g c) -> p g c", g=2).unsqueeze(3)
                                    .to_broadcast([P, 2, 2, HD]), ALU.mult)
                    V.tensor_tensor(heads(st[:, 256:384], 2), heads(PS[:, b0, 256:384], 2),
                                    stat[:, 42:44].unsqueeze(2).to_broadcast([P, 2, HD]),
                                    ALU.mult).then_inc(p_qs, 1)
                    dve.wait_ge(p_qs, NT * l + t + 1)
                    fin = None
                    for i, h0, h1 in ((0, 0, 4), (1, 4, 6)):
                        seg = heads(st[:, h0 * HD:h1 * HD], h1 - h0)
                        fin = V.tensor_tensor(seg, seg, head_g[:, i, :].unsqueeze(1).to_broadcast([P, h1 - h0, HD]),
                                              ALU.mult)
                    if t == LT:
                        fin.then_inc(ra_done, 1)
                        return
                    link(fin)
                    x4 = st.rearrange("p (h d two) -> p h d two", h=6, two=2)
                    s4 = ra2.rearrange("p (h d two) -> p h d two", h=6, two=2)
                    ts = rope_a[:, t, 1, :].rearrange("p (d two) -> p d two", two=2)
                    V.tensor_tensor(heads(ra1, 6), heads(st, 6),
                                    rope_a[:, t, 0, :].unsqueeze(1).to_broadcast([P, 6, HD]), ALU.mult)
                    for a in range(2):
                        fin = V.tensor_tensor(s4[:, :, :, a], x4[:, :, :, 1 - a],
                                              ts[:, :, a].unsqueeze(1).to_broadcast([P, 6, HD // 2]), ALU.mult)
                    link(fin)
                    V.tensor_tensor(st, ra1, ra2, ALU.add).then_inc(ra_done, 1)

                def step_q(l, t):
                    dve.wait_ge(q_T, NT * l + t + 1)
                    V.tensor_copy(qkT[:, 4:7, t * P:(t + 1) * P],
                                  PS[:, 1, 0:384].rearrange("p (c n) -> p c n", c=3)).then_inc(b1_evac, 1)

                def step_f(l, n):
                    if n not in (3, 5):
                        return
                    i = (n - 3) // 2
                    src = pair(2 + 2 * (n % 3), TOK)
                    dve.wait_ge(f_mm, 6 * l + n + 1)
                    dve.wait_ge(f_act, 4 * l + 3 + i)
                    V.tensor_tensor(u[:, i, PAD:PAD + LAT], src[:, 0:LAT], sig[:, 0:LAT], ALU.mult)
                    V.tensor_tensor(u[:, i, CTX0:CTX0 + CTX], src[:, LAT:TOK], sig[:, LAT:TOK],
                                    ALU.mult).then_inc(f_u, 1)

                normalise(l, 0)
                normalise(l, 1)
                for kind, n in ORDER:
                    if kind == "x":
                        step_x(l, n)
                    elif kind == "s":
                        normalise(l, n)
                    elif kind == "j":
                        step_j(l, n)
                    elif kind == "q":
                        step_q(l, n)
                    elif kind == "f":
                        step_f(l, n)
                finish_phase(l, 2)

                def maximum(l, n):
                    uu = unit_of(n)
                    t, gqa, h, n0 = head(uu)
                    w = TOK if t < LT else P
                    dve.wait_ge(t_scores, NT * MAPS * l + n + 1)
                    link(V.reduce_max(stat[:, 44 + n % 2:45 + n % 2], pair(2 * (n % 2), w), AX.X))
                    if n >= 4:
                        dve.wait_ge(t_exp, NT * MAPS * l + n - 3)
                    V.tensor_scalar(stat[:, 8 + n % 4:9 + n % 4], stat[:, 44 + n % 2:45 + n % 2],
                                    -(HD ** -0.5) if gqa else -(32 ** -0.5), None, ALU.mult).then_inc(t_max, 1)

                def combine(l, uu):
                    t, gqa, h, n0 = head(uu)
                    w = TOK if t < LT else P
                    n = maps_of(uu)[-1]
                    dve.wait_ge(t_exp, NT * MAPS * l + n + 1)
                    if gqa:
                        r0 = 64 + 4 * (t % 2) + h
                        V.reciprocal(stat[:, r0:r0 + 1], stat[:, 12 + n % 4:13 + n % 4])
                        return
                    link(V.reciprocal(stat[:, 48:50], stat[:, 12 + n0 % 4:14 + n0 % 4]))
                    V.tensor_scalar(stat[:, 50:51], stat[:, 49:50], lams[:, 5:6], None, ALU.mult)
                    link(V.tensor_scalar(Pm[:, n0 % 3, 0:w], Pm[:, n0 % 3, 0:w], stat[:, 48:49], None, ALU.mult))
                    V.scalar_tensor_tensor(Pm[:, n % 3, 0:w], Pm[:, n % 3, 0:w], stat[:, 50:51],
                                           Pm[:, n0 % 3, 0:w], ALU.mult, ALU.add).then_inc(t_comb, 1)

                def sub_norm(l, t):
                    dve.wait_ge(t_od, NT * l + t + 1)
                    diff = o_raw[:, 256:512]
                    if t >= 1:
                        dve.wait_ge(t_oT, NT * l + t)
                    link(V.tensor_tensor(osq, diff, diff, ALU.mult))
                    V.tensor_reduce(stat[:, 52:56], heads(osq, 4), AX.X, ALU.add).then_inc(t_dss, 1)
                    V.tensor_tensor(heads(o_tok[:, 0:256], 4), heads(o_raw[:, 0:256], 4),
                                    stat[:, 64 + 4 * (t % 2):68 + 4 * (t % 2)].unsqueeze(2)
                                    .to_broadcast([P, 4, HD]), ALU.mult)
                    dve.wait_ge(t_dr, NT * l + t + 1)
                    link(V.tensor_tensor(heads(osq, 4), heads(diff, 4),
                                         stat[:, 56:60].unsqueeze(2).to_broadcast([P, 4, HD]), ALU.mult))
                    V.tensor_tensor(heads(o_tok[:, 256:512], 4), heads(osq, 4),
                                    subg[:, :].unsqueeze(1).to_broadcast([P, 4, HD]), ALU.mult).then_inc(t_otok, 1)

                def conv_tap(k):
                    if k == 0:
                        link(V.tensor_scalar(y3[:, 0, :], u[:, 0, 0:OUTW], cwT[:, 0, 0:1], pT[:, 18:19],
                                             ALU.mult, ALU.add))
                    else:
                        link(V.scalar_tensor_tensor(y3[:, 0, :], u[:, 0, k:k + OUTW], cwT[:, 0, k:k + 1],
                                                    y3[:, 0, :], ALU.mult, ALU.add))

                maximum(l, 0)
                for uu in range(STEPS + 3):
                    if uu < STEPS:
                        combine(l, uu)
                    if uu + 1 < STEPS:
                        for n in maps_of(uu + 1):
                            maximum(l, n)
                    if uu < TAPS:
                        conv_tap(uu)
                    if uu >= UNITS + 1 and (uu - 1) % UNITS == 0:
                        sub_norm(l, (uu - 1) // UNITS - 1)
                finish_phase(l, 3)

                dve.wait_ge(c_mean, l + 1)
                for i in range(2):
                    V.tensor_tensor(y3[:, i, :], y3[:, i, :], pair(4, OUTW), ALU.subtract).then_inc(c_yc, 1)
                dve.wait_ge(c_var, l + 1)
                V.tensor_scalar(rstd_y, pair(6, OUTW), EPS, None, ALU.add).then_inc(c_vs, 1)
                dve.wait_ge(c_rs, l + 1)
                for i in range(2):
                    V.tensor_tensor(y3[:, i, :], y3[:, i, :], rstd_y, ALU.mult).then_inc(c_yn, 1)
                finish_phase(l, 4)

                dve.wait_ge(g_loaded, 64 * (l + 1))

                def residual(l, t):
                    dve.wait_ge(o_mm, NT * l + t + 1)
                    V.tensor_tensor(gated, pair(2 * (t % 2)), gb1[:, 0 if t < LT else 1, :],
                                    ALU.mult).then_inc(o_g, 1)
                    dve.wait_ge(o_g, NT * l + t + 1)
                    dve.wait_ge(xo_loaded[t % 2], 16 * parity_count(l, t))
                    V.tensor_tensor(xo[:, t % 2, :], xo[:, t % 2, :], gated, ALU.add).then_inc(o_x, 1)

                residual(l, 0)
                for t in range(NT):
                    dve.wait_ge(o_r, NT * l + t + 1)
                    if t >= 2:
                        dve.wait_ge(o_xT, NT * l + t - 1)
                        dve.wait_ge(x_saved[t % 2], 32 * parity_count(l, t - 2))
                    V.tensor_scalar(xnb[:, t % 2, :], xo[:, t % 2, :], stat[:, 24 + t:25 + t], None,
                                    ALU.mult).then_inc(o_xn, 1)
                    dve.wait_ge(o_xT, NT * l + t + 1)
                    v = 0 if t < LT else 1
                    for j in range(4):
                        last = V.tensor_scalar(H[:, 4 + j, t * P:(t + 1) * P], PS[:, 5, j * P:(j + 1) * P],
                                               modA[:, 1, v, 4 + j:5 + j], modB[:, 1, v, 4 + j:5 + j],
                                               ALU.mult, ALU.add)
                    last.then_inc(o_h5, 1)
                    if t + 1 < NT:
                        residual(l, t + 1)
                dve.wait_ge(o_lg, NT * (l + 1))
                lg3 = PS[:, 6, 0:80].rearrange("p (t e) -> p t e", t=NT)
                link(V.reduce_max(stat[:, 32:37], lg3, AX.X))
                V.tensor_tensor(logit.rearrange("p (t e) -> p t e", t=NT), lg3,
                                stat[:, 32:37].unsqueeze(2).to_broadcast([P, NT, EXPERTS]),
                                ALU.subtract).then_inc(r_sub, 1)
                dve.wait_ge(r_exp, l + 1)
                link(V.tensor_reduce(stat[:, 38:43], logit.rearrange("p (t e) -> p t e", t=NT), AX.X, ALU.add))
                link(V.reciprocal(stat[:, 32:37], stat[:, 38:43]))
                V.tensor_tensor(aff.rearrange("p (t e) -> p t e", t=NT), logit.rearrange("p (t e) -> p t e", t=NT),
                                stat[:, 32:37].unsqueeze(2).to_broadcast([P, NT, EXPERTS]),
                                ALU.mult).then_inc(r_aff, 1)
                wait_apart(dve, r_affs, l + 1)
                for lo, hi, s0, n in ((0, LAT, 0, CAPL), (LAT, TOK, CAPL, CAPC)):
                    row = affT[0:EXPERTS, lo:hi]
                    for i in range(n // 8):
                        s = slice(s0 + 8 * i, s0 + 8 * i + 8)
                        link(V.max(topv[0:EXPERTS, s], row), bare=True)
                        V.max_index(topi[0:EXPERTS, s], topv[0:EXPERTS, s], row)
                        link(V.match_replace(row, topv[0:EXPERTS, s], row, -1.0), bare=True)
                link(V.tensor_copy(topf[0:EXPERTS, :], topi[0:EXPERTS, :]))
                V.tensor_scalar(topf[0:EXPERTS, CAPL:CAP], topf[0:EXPERTS, CAPL:CAP], float(LAT), None,
                                ALU.add).then_inc(k_top, 1)
                dve.wait_ge(k_T, l + 1)
                V.tensor_copy(idxT[0:CAP, 0:EXPERTS], PS[0:CAP, 0, 0:EXPERTS])
                V.tensor_copy(idxT[0:CAP, EXPERTS:EXPERTS + 1], PS[0:CAP, 0, 0:1])
                V.tensor_copy(gateT[0:CAP, 0:EXPERTS], PS[0:CAP, 0, 16:16 + EXPERTS])
                finish_phase(l, 5)

                V.tensor_copy(idxc[0:CAP, 0:1], idxT[0:CAP, 0:1]).then_inc(e_idx, 1)

                def expert(l, e, p):
                    done = l * EXPERTS + e
                    rnd = l * ROUNDS + 3 + e
                    dve.wait_ge(rows_added, done + CREDIT)
                    V.tensor_copy(gatec[0:CAP, :], gateT[0:CAP, bass.ds(e, 1)])
                    V.tensor_copy(idxc[0:CAP, 1 - p:2 - p], idxT[0:CAP, bass.ds(e + 1, 1)]).then_inc(e_idx, 1)

                    def hidden(c):
                        dve.wait_ge(e_sil, 2 * done + 1 + c + CREDIT)
                        V.tensor_tensor(hid[0:CAP, c * 512:(c + 1) * 512], sil[0:CAP, c * 512:(c + 1) * 512],
                                        PS[0:CAP, 2 + c, :], ALU.mult).then_inc(e_hid, 1)

                    def take_hidden(c, turned, done_sem):
                        dve.wait_ge(turned, done + 1)
                        V.tensor_copy(hidT[:, 4 * c:4 * c + 4, :].rearrange("p j n -> p (j n)"),
                                      PS[:, 6 + c, 0:4 * CAP]).then_inc(done_sem, 1)

                    dve.wait_ge(e_U0, done + 1)
                    hidden(0)
                    take_hidden(0, e_T0, e_hT0)
                    dve.wait_ge(slot_used[3], rnd + 1 + CREDIT)
                    hidden(1)
                    take_hidden(1, e_T1, e_hT1)
                    dve.wait_ge(slot_used[5], rnd + 1 + CREDIT)
                    V.scalar_tensor_tensor(yb[0:CAP, :], pair(4)[0:CAP, :], gatec[0:CAP, :], g2b[0:CAP, :],
                                           ALU.mult, ALU.mult).then_inc(e_y, 1)

                with dve.Fori(0, EXPERTS // 2) as e2:
                    expert(l, 2 * e2, 0)
                    expert(l, 2 * e2 + 1, 1)
                finish_phase(l, 6)
            assert chain[0] == V_LINKS, ("V_LINKS", chain[0])

            dve.wait_ge(fin_g, 16)
            for t in range(NT):
                dve.wait_ge(fin_r, t + 1)
                V.scalar_tensor_tensor(xo[:, t % 2, :], xo[:, t % 2, :], stat[:, 24 + t:25 + t], fgb,
                                       ALU.mult, ALU.mult).then_inc(fin_y, 1)

        @block.gpsimd
        def _(pool):
            G = nc.gpsimd
            pool.sem_inc(rows_added, CREDIT)
            chain = [0, 0]

            def reach(semaphore, value):
                wait_apart(pool, semaphore, value)

            def link(ins_):
                chain[0] += 1
                ins_.then_inc(pool_chain, 1)
                reach(pool_chain, chain[1] + chain[0])

            def finish_phase(l, k):
                pool.drain().then_inc(phase_done, 1)
                reach(phase_done, 4 * (l * PHASES + k))

            def rsqrt_mean(out, sums, n, count, done):
                link(G.tensor_scalar(out, sums, 1.0 / count, EPS, ALU.mult, ALU.add))
                G.tensor_tensor(out, out, neghalf[:, :].to_broadcast([P, n]), ALU.pow).then_inc(done, 1)

            G.memset(mean_w[:, :], 1.0 / 256).then_inc(consts_set, 1)
            G.memset(pool_w[:, :, :], 0.0).then_inc(consts_set, 1)
            reach(const_loaded, 16 * N_CONST)

            with pool.Fori(0, LAYERS) as l:
                chain[0], chain[1] = 0, l * G_LINKS
                finish_phase(l, 1)

                for i, lo, hi in ((0, 0, PAD), (0, PAD + LAT, CTX0), (0, CTX0 + CTX, SEQW)):
                    G.memset(poolT[:, :, lo:hi], 0.0)
                    last = G.memset(u[:, :, lo:hi], 0.0)
                last.then_inc(pads_zero, 1)

                def norm_stat(l, t):
                    reach(n_ss, NT * l + t + 1)
                    rsqrt_mean(stat[:, 24 + t:25 + t], stat[:, t:t + 1], 1, D, n_rstd)

                def step_j(l, t):
                    reach(p_ms, NT * l + t + 1)
                    if t >= 1:
                        reach(p_qs, NT * l + t)
                    rsqrt_mean(stat[:, 38:44], stat[:, 32:38], 6, HD, p_r)
                    if t == LT:
                        return
                    reach(p_ds, NT * l + t + 1)
                    st = stage[:, t % 2, 384:896]
                    x4 = st.rearrange("p (h d two) -> p h d two", h=16, two=2)
                    s4 = rd2.rearrange("p (h d two) -> p h d two", h=16, two=2)
                    ts = rope_d[:, t, 1, :].rearrange("p (d two) -> p d two", two=2)
                    G.tensor_tensor(rd1.rearrange("p (h d) -> p h d", h=16), st.rearrange("p (h d) -> p h d", h=16),
                                    rope_d[:, t, 0, :].unsqueeze(1).to_broadcast([P, 16, 32]), ALU.mult)
                    for a in range(2):
                        fin = G.tensor_tensor(s4[:, :, :, a], x4[:, :, :, 1 - a],
                                              ts[:, :, a].unsqueeze(1).to_broadcast([P, 16, 16]), ALU.mult)
                    link(fin)
                    G.tensor_tensor(st, rd1, rd2, ALU.add).then_inc(rd_done, 1)

                norm_stat(l, 0)
                norm_stat(l, 1)
                for kind, n in ORDER:
                    if kind == "s":
                        norm_stat(l, n)
                    elif kind == "j":
                        step_j(l, n)
                finish_phase(l, 2)

                reach(pads_zero, l + 1)
                half = slice(HD, P)
                for i in range(2):
                    x = poolT[:, i, :]
                    link(G.tensor_tensor(wa[:, 1:SEQW], x[:, 0:SEQW - 1], x[:, 1:SEQW], ALU.add))
                    if i == 0:
                        link(G.tensor_tensor(wb[half, 2:SEQW - 1], wa[half, 1:SEQW - 2], wa[half, 3:SEQW], ALU.add))
                    else:
                        link(G.tensor_tensor(wb[:, 2:SEQW - 1], wa[:, 1:SEQW - 2], wa[:, 3:SEQW], ALU.add))
                        link(G.tensor_tensor(wa[:, 4:SEQW - 3], wb[:, 2:SEQW - 5], wb[:, 6:SEQW - 1], ALU.add))
                        link(G.tensor_tensor(wb[half, 8:SEQW - 7], wa[half, 4:SEQW - 11], wa[half, 12:SEQW - 3],
                                             ALU.add))
                    for rows, src in ((slice(0, HD), wa), (half, wb)):
                        last = G.tensor_scalar(poolD3[rows, i, :], src[rows, PAD:PAD + OUTW], invw[rows, i:i + 1],
                                               None, ALU.mult)
                    link(last)
                    for c0, n in ((0, LAT), (CTX0 - PAD, CTX)):
                        for side in range(2):
                            c = c0 + side * (n - 8)
                            ends = poolD3[:, i, c:c + 8]
                            last = G.tensor_tensor(ends, ends, edge[:, i, side, :], ALU.mult)
                    link(last)
                    link(G.tensor_tensor(poolD3[:, i, :], poolD3[:, i, :], x[:, PAD:PAD + OUTW], ALU.subtract))

                per_tile = TAPS // NT
                for k in range(TAPS):
                    if k == 0:
                        link(G.tensor_scalar(y3[:, 1, :], u[:, 1, 0:OUTW], cwT[:, 1, 0:1], pT[:, 19:20],
                                             ALU.mult, ALU.add))
                    else:
                        link(G.tensor_scalar(tap, u[:, 1, k:k + OUTW], cwT[:, 1, k:k + 1], None, ALU.mult))
                        link(G.tensor_tensor(y3[:, 1, :], y3[:, 1, :], tap, ALU.add))
                    if k % per_tile == per_tile - 1 and k // per_tile < NT:
                        reach(t_dss, NT * l + k // per_tile + 1)
                        rsqrt_mean(stat[:, 56:60], stat[:, 52:56], 4, HD, t_dr)
                finish_phase(l, 3)

                reach(c_vs, l + 1)
                G.tensor_tensor(rstd_y, rstd_y, neghalf[:, :].to_broadcast([P, OUTW]), ALU.pow).then_inc(c_rs, 1)
                finish_phase(l, 4)

                for t in range(NT):
                    reach(o_ss, NT * l + t + 1)
                    rsqrt_mean(stat[:, 24 + t:25 + t], stat[:, 16 + t:17 + t], 1, D, o_r)
                finish_phase(l, 5)

                def gather(p):
                    pool.indirect_dma_start(xg[0:CAP, p, :], None, xn_dram[:, :],
                                            bass.IndirectOffsetOnAxis(ap=idxc[0:CAP, p:p + 1], axis=0))\
                        .then_inc(e_gath[p], 16)

                reach(e_idx, 17 * l + 1)
                gather(0)

                def expert(l, e, p):
                    done = l * EXPERTS + e
                    reach(e_idx, 17 * l + e + 2)
                    reach(e_X1, 17 * l + e + 1)
                    gather(1 - p)
                    reach(e_y, done + 1 + CREDIT)
                    pool.indirect_dma_start(x_dram[:, :], bass.IndirectOffsetOnAxis(ap=idxc[0:CAP, p:p + 1], axis=0),
                                            yb[0:CAP, :], None, compute_op=ALU.add).then_inc(e_scat, 16)
                    pool.wait_ge(e_scat, 16 * (done + 1))
                    pool.sem_inc(rows_added, 1)

                with pool.Fori(0, EXPERTS // 2) as e2:
                    expert(l, 2 * e2, 0)
                    expert(l, 2 * e2 + 1, 1)
                finish_phase(l, 6)
            assert chain[0] == G_LINKS, ("G_LINKS", chain[0])

            for t in range(NT):
                reach(fin_ss, t + 1)
                last = rsqrt_mean(stat[:, 24 + t:25 + t], stat[:, 16 + t:17 + t], 1, D, fin_r)


V_LINKS = 176
G_LINKS = 97
ORDER = (("x", 0), ("s", 2), ("x", 1), ("j", 0), ("s", 3), ("x", 2), ("j", 1), ("q", 0), ("s", 4), ("x", 3), ("j", 2),
         ("q", 1), ("x", 4), ("j", 3), ("q", 2), ("j", 4), ("q", 3), ("f", 0), ("q", 4), ("f", 1), ("f", 2),
         ("f", 3), ("f", 4), ("f", 5))
_BANK_USES = [step for step in ORDER if step[0] in "xq"]
XUSE = {n: i for i, (kind, n) in enumerate(_BANK_USES) if kind == "x"}
FCHUNK = ((0, 512), (0, 640), (2, 0), (0, 768), (2, 128), (0, 896))


def shape_constants():
    f = np.float32

    def rope(dim):
        rows = np.repeat(np.arange(8), 64).astype(f)
        cols = np.tile(np.arange(64), 8).astype(f)
        quarter = dim // 4
        inv = f(10000.0) ** (-np.arange(quarter, dtype=f) / f(quarter))
        ang = np.concatenate([rows[:, None] * inv, cols[:, None] * inv], axis=-1)
        c, s = np.cos(ang).astype(f), np.sin(ang).astype(f)
        both = np.empty((512, 2, dim), f)
        both[:, 0, 0::2], both[:, 0, 1::2] = c, c
        both[:, 1, 0::2], both[:, 1, 1::2] = -s, s
        return both

    edge, invw = np.ones((128, 2, 2, 8), f), np.empty((128, 2), f)
    for g, w in enumerate((2, 4, 8, 16)):
        rows = slice(64 * (g % 2), 64 * (g % 2) + 64)
        invw[rows, g // 2] = 1.0 / w
        for t in range(8):
            edge[rows, g // 2, 0, t] = w / (min(t, w // 2) + w - w // 2)
            edge[rows, g // 2, 1, t] = w / (w // 2 + min(w - w // 2, 8 - t))
    lam = [0.8 - 0.6 * float(np.exp(-0.3 * n)) for n in range(2)]
    return {"k_ident": np.eye(128, dtype=f), "k_rope_a": rope(64), "k_rope_d": rope(32), "k_edge": edge,
            "k_invw": invw, "k_neghalf": np.full((128, 1), -0.5, f),
            "k_lam": np.array([[x, 1.0 - x] for x in lam], f)}


_OUTS = {"y_prompt": (1, 128, 1024), "y_sample": (1, 512, 1024), "state_gqa_k": (1, 2, 128, 2, 64),
         "state_gqa_v": (1, 2, 128, 2, 64), "state_diff_k": (1, 2, 128, 4, 64), "state_diff_v": (1, 2, 128, 4, 64)}


def kernel(**inputs):
    import concourse.bacc as _bacc
    from concourse.bass_utils import run_bass_kernel_spmd as _run

    nc = _bacc.Bacc("TRN2", target_bir_lowering=False, num_devices=1)
    arrays, ins, outs = {}, {}, {}
    for name, a in {**inputs, **shape_constants()}.items():
        a = np.ascontiguousarray(a)
        arrays[f"in_{name}"] = a
        ins[name] = nc.dram_tensor(f"in_{name}", a.shape, mybir.dt.from_np(a.dtype), kind="ExternalInput").ap()
    for name, shape in _OUTS.items():
        outs[name] = nc.dram_tensor(f"out_{name}", shape, mybir.dt.float32, kind="ExternalOutput").ap()
    backbone_step_kernel(nc, ins, outs)
    r = _run(nc, [arrays], core_ids=[0])
    return tuple(r.results[0][f"out_{name}"] for name in _OUTS)
```

```python
import concourse.bass as bass
from concourse import mybir
from contextlib import ExitStack

import numpy as np


def backbone_step_kernel(nc, ins, outs):
    F32, U32, BF16 = mybir.dt.float32, mybir.dt.uint32, mybir.dt.bfloat16
    ALU, ACT, AX = mybir.AluOpType, mybir.ActivationFunctionType, mybir.AxisListType

    P = 128
    D = 1024
    LAT, CTX = 512, 128
    TOK = LAT + CTX
    NT = TOK // P
    LT = LAT // P
    KD = D // P
    LAYERS = 2
    EXPERTS = 16
    CAPL, CAPC = 2 * LAT // EXPERTS, 2 * CTX // EXPERTS
    CAP = CAPL + CAPC
    HD = 64
    EPS = 1e-6
    TAPS, PAD = 31, 15
    SEQW = PAD + LAT + PAD + CTX + PAD
    CTX0 = PAD + LAT + PAD
    OUTW = SEQW - 2 * PAD
    ROUNDS = 3 + EXPERTS
    PHASES = 6

    ctx = ExitStack()
    with ctx:
        def sb(name, shape, dt=F32):
            return ctx.enter_context(nc.sbuf_tensor(name, shape, dt))

        def sem(name):
            return ctx.enter_context(nc.semaphore(name))

        ring = sb("ring", [P, 6, 4, D])
        H = sb("H", [P, KD, TOK])
        ident = sb("ident", [P, P])
        mean_w = sb("mean_w", [P, P])
        neghalf = sb("neghalf", [P, 1])
        rope_a = sb("rope_a", [P, LT, 2, HD])
        rope_d = sb("rope_d", [P, LT, 2, HD // 2])
        edge = sb("edge", [P, 2, 2, 8])
        invw = sb("invw", [P, 2])
        rows_of = sb("rows_of", [P, 6])
        crow = sb("crow", [16, P])
        scT = sb("scT", [P, KD, 32])
        pT = sb("pT", [P, 72])
        mod = sb("mod", [P, 6, KD, 2])
        cwT = sb("cwT", [P, 2, 32])
        head_g = sb("head_g", [P, 3, HD])
        subg = sb("subg", [P, HD])
        lamv = sb("lamv", [P, 4, 32])
        lamc = sb("lamc", [P, 2])
        lamw = sb("lamw", [P, 2, 32])
        lams = sb("lams", [P, 8])
        router = sb("router", [P, KD, EXPERTS])
        pool_w = sb("pool_w", [P, 2, P])
        conv_pw = sb("conv_pw", [P, 2, 2 * P])
        cv = sb("cv", [P, 384])
        kcT = sb("kcT", [P, 3, P])
        modA = sb("modA", [P, 2, 2, KD])
        modB = sb("modB", [P, 2, 2, KD])
        stat = sb("stat", [P, 112])
        gate_rows = sb("gate_rows", [32, P])

        ARENA = 18890
        arena = sb("arena", [P, ARENA])
        at = [0]

        def carve(words):
            v = arena[:, at[0]:at[0] + words]
            at[0] += words
            assert at[0] <= ARENA, at[0]
            return v

        qkT = carve(7 * TOK).rearrange("p (c n) -> p c n", c=7)
        vA = carve(NT * P).rearrange("p (t n) -> p t n", t=NT)
        vD = carve(NT * 2 * P).rearrange("p (t n) -> p t n", t=NT)
        stage = carve(2 * 896).rearrange("p (b n) -> p b n", b=2)
        soft = carve(3200)
        Pm = soft[:, 0:1920].rearrange("p (b n) -> p b n", b=3)
        PT = soft[:, 1920:3200].rearrange("p (b n) -> p b n", b=2)
        ra1, ra2, rd1, rd2 = soft[:, 0:384], soft[:, 384:768], soft[:, 768:1280], soft[:, 1280:1792]
        qsq = soft[:, 1792:2176]
        ck, prow, cwrow = soft[:, 0:384], soft[0:72, 384:384 + P], soft[0:TAPS, 512:768]
        gate_cols = soft[:, 768:800]
        o_raw = stage[:, 1, 0:768]
        o_tok = carve(512)
        osq = carve(256)
        junk = o_tok.bitcast(BF16)
        poolT = carve(2 * SEQW).rearrange("p (i n) -> p i n", i=2)
        u = carve(2 * SEQW).rearrange("p (i n) -> p i n", i=2)
        y = carve(2 * OUTW)
        y3 = y.rearrange("p (i n) -> p i n", i=2)
        wa = carve(SEQW)
        wb = carve(SEQW)
        poolD = carve(2 * OUTW)
        poolD3 = poolD.rearrange("p (i n) -> p i n", i=2)
        sig, tap = wa[:, 0:TOK], wa[:, 0:OUTW]
        ysq = poolT.rearrange("p i n -> p (i n)")[:, 0:2 * OUTW].rearrange("p (i n) -> p i n", i=2)
        rstd_y = wb[:, 0:OUTW]
        xt = [poolD[:, 0:D], y[:, 0:D]]
        modrow = arena[:, 0:6 * D // 4].rearrange("p (b n) -> p b n", b=6)
        at[0] = 0
        gb1 = carve(2 * D).rearrange("p (v n) -> p v n", v=2)
        xo = carve(2 * D).rearrange("p (b n) -> p b n", b=2)
        xnb = carve(2 * D).rearrange("p (b n) -> p b n", b=2)
        gated = carve(D)
        junk2 = carve(D // 2).bitcast(BF16)
        logit = carve(80)
        aff = carve(80)
        affT = carve(TOK)
        topv = carve(80)
        topi = carve(80).bitcast(U32)
        topf = carve(80)
        gateT = carve(17)
        idxT = carve(17).bitcast(U32)
        idxc = carve(2).bitcast(U32)
        gatec = carve(1)
        g2b = carve(D)
        xg = carve(2 * D).rearrange("p (b n) -> p b n", b=2)
        xeT = carve(KD * CAP).rearrange("p (j n) -> p j n", j=KD)
        sil = carve(D)
        hid = carve(D)
        hidT = carve(KD * CAP).rearrange("p (j n) -> p j n", j=KD)
        yb = carve(D)
        fgb = gb1[:, 0, :]
        xf = arena[:, 2 * D:(2 + NT) * D].rearrange("p (t n) -> p t n", t=NT)

        PS = ctx.enter_context(nc.psum_tensor("PS", [P, 8, 512], F32))
        flat = PS[:, :, :].rearrange("p b n -> p (b n)")

        def pair(b, n=D):
            return flat[:, b * 512:b * 512 + n]

        x_dram = nc.dram_tensor("x_rows", [TOK, D], F32, kind="Internal").ap()
        xn_dram = nc.dram_tensor("xn_rows", [TOK, D], F32, kind="Internal").ap()
        modg = nc.dram_tensor("mod_gates", [2, 2, D], F32, kind="Internal").ap()

        const_loaded, x_seeded = sem("const_loaded"), sem("x_seeded")
        params_loaded = sem("params_loaded")
        slot_ready = [sem(f"slot_ready{s}") for s in range(6)]
        slot_used = [sem(f"slot_used{s}") for s in range(6)]
        phase_done = sem("phase_done")
        c_turned, silu_c = sem("c_turned"), sem("silu_c")
        tensor_chain = sem("vector_chain")
        pool_chain = sem("pool_chain")
        consts_set = sem("consts_set")
        waits_passed = sem("waits_passed")
        mod_taken, mod_turned, params_turned = sem("mod_taken"), sem("mod_turned"), sem("params_turned")
        gates_picked, gates_turned, gates_taken = sem("gates_picked"), sem("gates_turned"), sem("gates_taken")
        kc_turned = sem("kc_turned")
        gates_saved = sem("gates_saved")
        lam_sums, lam_exps = sem("lam_sums"), sem("lam_exps")
        x_loaded = [sem("x_loaded0"), sem("x_loaded1")]
        n_ss, n_rstd, n_xn, n_xT = sem("n_ss"), sem("n_rstd"), sem("n_xn"), sem("n_xT")
        b0_evac, b1_evac = sem("b0_evac"), sem("b1_evac")
        p_mm, p_sq, p_ds, p_v, p_qs = sem("p_mm"), sem("p_sq"), sem("p_ds"), sem("p_v"), sem("p_qs")
        p_ms, p_r = sem("p_ms"), sem("p_r")
        ra_done, rd_done, q_T = sem("ra_done"), sem("rd_done"), sem("q_T")
        f_mm, f_act, f_u = sem("f_mm"), sem("f_act"), sem("f_u")
        pads_zero = sem("pads_zero")
        state_saved = sem("state_saved")
        t_scores, t_max, t_exp = sem("t_scores"), sem("t_max"), sem("t_exp")
        t_pT, t_pt, t_pv, t_taken = sem("t_pT"), sem("t_pt"), sem("t_pv"), sem("t_taken")
        t_dss, t_dr, t_otok = sem("t_dss"), sem("t_dr"), sem("t_otok")
        t_oT, t_oTe = sem("t_oT"), sem("t_oTe")
        q_spread, c_y = sem("q_spread"), sem("c_y")
        c_mix, c_mean, c_yc, c_sq, c_var = sem("c_mix"), sem("c_mean"), sem("c_yc"), sem("c_sq"), sem("c_var")
        c_vs, c_rs, c_yn, c_z, c_pw, c_mixe = (sem("c_vs"), sem("c_rs"), sem("c_yn"), sem("c_z"), sem("c_pw"),
                                               sem("c_mixe"))
        g_loaded = sem("g_loaded")
        xo_loaded = [sem("xo_loaded0"), sem("xo_loaded1")]
        x_saved = [sem("x_saved0"), sem("x_saved1")]
        o_mm, o_g, o_x, o_ss, o_r, o_xn = sem("o_mm"), sem("o_g"), sem("o_x"), sem("o_ss"), sem("o_r"), sem("o_xn")
        o_xT, o_h4, o_h5, o_lg = sem("o_xT"), sem("o_h4"), sem("o_h5"), sem("o_lg")
        r_sub, r_exp, r_aff, r_affT, r_affs = (sem("r_sub"), sem("r_exp"), sem("r_aff"), sem("r_affT"),
                                               sem("r_affs"))
        k_top, k_T = sem("k_top"), sem("k_T")
        e_idx = sem("e_idx")
        e_gath = [sem("e_gath0"), sem("e_gath1")]
        e_X0, e_X1, e_xe = sem("e_X0"), sem("e_X1"), sem("e_xe")
        e_sil, e_U0, e_hid = sem("e_sil"), sem("e_U0"), sem("e_hid")
        e_T0, e_T1, e_hT0, e_hT1 = sem("e_T0"), sem("e_T1"), sem("e_hT0"), sem("e_hT1")
        e_y, e_scat, rows_added = sem("e_y"), sem("e_scat"), sem("rows_added")
        fin_x = [sem(f"fin_x{t}") for t in range(NT)]
        fin_g, fin_ss, fin_r, fin_y = sem("fin_g"), sem("fin_ss"), sem("fin_r"), sem("fin_y")
        fin_saved = sem("fin_saved")

        CREDIT = 1

        block = ctx.enter_context(nc.Block())

        def wait_apart(eng, semaphore, value):
            eng.wait_ge(semaphore, value)
            eng.sem_inc(waits_passed, 1)

        N_PARAMS = 26
        N_CONST = 9
        X_LOADS = (3, 2)
        MAPS = 12
        NM = NT * MAPS
        OUT_AT = 15
        DVE_TAPS = 16

        def parity_count(l, t):
            return l * X_LOADS[t % 2] + t // 2 + 1

        def score_map(n):
            t, r = divmod(n, MAPS)
            return (t, True, r, 0) if r < 4 else (t, False, (r - 4) // 2, r % 2)

        SPREADS, SPREAD_BUFS = NM // 4, 5

        def spread_queries(g):
            free = H[:, 2:6, :].rearrange("p c n -> p (c n)").rearrange("p (b m n) -> p b m n", b=SPREAD_BUFS, m=4)
            return free[:, g % SPREAD_BUFS, :, :]

        def out_slot(n):
            t, gqa, h, m = score_map(n)
            return h if gqa else 4 + 4 * m + h

        @block.sync
        def _(sp):
            for dst, src in ((ident[:, :], ins["k_ident"]),
                             (rope_a[:, :, :, :], ins["k_rope_a"].rearrange("(t p) a n -> p t a n", p=P)),
                             (rope_d[:, :, :, :], ins["k_rope_d"].rearrange("(t p) a n -> p t a n", p=P)),
                             (edge[:, :, :, :], ins["k_edge"]),
                             (invw[:, :], ins["k_invw"]),
                             (rows_of[:, :], ins["k_rows_of"]),
                             (crow[0:8, :], ins["c"].rearrange("a (j p) -> (a j) p", p=P)),
                             (crow[8:16, :], ins["c_ctx"].rearrange("(j p) -> j p", p=P)),
                             (neghalf[:, :], ins["k_neghalf"])):
                sp.dma_start(dst, src).then_inc(const_loaded, 16)

            def slot_load(l, rnd, s, src):
                sp.wait_ge(slot_used[s], l * ROUNDS + rnd + CREDIT)
                sp.dma_start(ring[:, s, :, :], src.rearrange("(k p) n -> p k n", p=P)).then_inc(slot_ready[s], 16)

            with sp.Fori(0, LAYERS) as l:
                for rnd in range(2):
                    for m in range(3):
                        b = 3 * rnd + m
                        for h in range(2):
                            slot_load(l, rnd, 2 * m + h,
                                      ins["w_mod"][l, h * 512:(h + 1) * 512, b * D:(b + 1) * D])
                for m in range(2):
                    for h in range(2):
                        slot_load(l, 2, 2 * m + h, ins["w_in"][l, h * 512:(h + 1) * 512, m * D:(m + 1) * D])
                for h in range(2):
                    slot_load(l, 2, 4 + h, ins["w_out"][l, h * 512:(h + 1) * 512, :])
                with sp.Fori(0, EXPERTS) as e:
                    for m, w in enumerate(("exp_w_gate", "exp_w_up", "exp_w_down")):
                        for h in range(2):
                            slot_load(l, 3 + e, 2 * m + h, ins[w][l, e, h * 512:(h + 1) * 512, :])

            sp.wait_ge(phase_done, 4 * LAYERS * PHASES)
            sp.dma_start(fgb, ins["final_g"].rearrange("(a n) -> a n", a=1).to_broadcast([P, D])).then_inc(fin_g, 16)
            for t in range(NT):
                sp.wait_ge(fin_y, t + 1)
                dst = outs["y_sample"][0, t * P:(t + 1) * P, :] if t < LT else outs["y_prompt"][0, :, :]
                sp.dma_start(dst, xf[:, t, :]).then_inc(fin_saved, 16)
            sp.wait_ge(fin_saved, 16 * NT)

        @block.tensor
        def _(pe):
            mm, tr = nc.tensor.matmul, nc.tensor.transpose
            for s in slot_used:
                pe.sem_inc(s, CREDIT)

            def finish_phase(l, k):
                pe.drain().then_inc(phase_done, 1)
                pe.wait_ge(phase_done, 4 * (l * PHASES + k))

            pe.wait_ge(const_loaded, 16 * N_CONST)
            tr(PS[:, 7, 0:16], crow[:, :], ident[0:16, 0:16]).then_inc(c_turned, 1)
            pe.wait_ge(silu_c, 1)
            pe.wait_ge(consts_set, 3)

            with pe.Fori(0, LAYERS) as l:
                def turn_mod(l, b):
                    pe.wait_ge(mod_taken, 6 * l + b + 1)
                    for i in range(2):
                        c0 = 2 * P * (b % 2) + P * i
                        last = tr(PS[:, 4 + b // 2, c0:c0 + P], modrow[:, b, i * P:(i + 1) * P], ident[:, :])
                    last.then_inc(mod_turned, 1)

                for b in range(6):
                    rnd, m = divmod(b, 3)
                    if b >= 3:
                        pe.wait_ge(mod_taken, 6 * l + b - 2)
                    for h in range(2):
                        pe.wait_ge(slot_ready[2 * m + h], 16 * (l * ROUNDS + rnd + 1))
                        for kk in range(4):
                            k = 4 * h + kk
                            for q in range(4):
                                last = mm(PS[32 * q:32 * q + 32, b % 3, 0:256], scT[:, k, :],
                                          ring[:, 2 * m + h, kk, q * 256:(q + 1) * 256],
                                          start=(k == 0), stop=(k == KD - 1))
                        last.then_inc(slot_used[2 * m + h], 1)
                    if b == 4:
                        pe.wait_ge(params_loaded, 16 * N_PARAMS * (l + 1))
                        for i in range(3):
                            last = tr(PS[:, 7, i * P:(i + 1) * P], ck[:, i * P:(i + 1) * P], ident[:, :])
                        last.then_inc(kc_turned, 1)
                        tr(PS[:, 3, 0:72], prow, ident[0:72, 0:72])
                        for i in range(2):
                            last = tr(PS[:, 3, 96 + 32 * i:96 + 32 * i + TAPS], cwrow[:, i * P:(i + 1) * P],
                                      ident[0:TAPS, 0:TAPS])
                        last.then_inc(params_turned, 1)
                    if b >= 1:
                        turn_mod(l, b - 1)
                turn_mod(l, 5)
                pe.wait_ge(gates_picked, l + 1)
                tr(PS[0:32, 0, 0:P], gate_cols, ident[:, :]).then_inc(gates_turned, 1)
                finish_phase(l, 1)

                uses = [0]

                def banks01(l):
                    if uses[0]:
                        pe.wait_ge(b0_evac, 10 * l + uses[0])
                        pe.wait_ge(b1_evac, 10 * l + uses[0])
                    uses[0] += 1

                def step_x(l, t):
                    pe.wait_ge(n_xn, NT * l + t + 1)
                    banks01(l)
                    for j in range(KD):
                        last = tr(PS[:, j // 4, (j % 4) * P:(j % 4 + 1) * P], xt[t % 2][:, j * P:(j + 1) * P],
                                  ident[:, :])
                    last.then_inc(n_xT, 1)

                def step_j(l, t):
                    pe.wait_ge(b0_evac, 10 * l + XUSE[t] + 1)
                    pe.wait_ge(b1_evac, 10 * l + XUSE[t] + 1)
                    if t >= 2:
                        pe.wait_ge(p_v, NT * l + t - 1)
                        pe.wait_ge(p_qs, NT * l + t - 1)
                    b0 = 2 + 3 * (t % 2)
                    if t == 0:
                        for s in range(4):
                            pe.wait_ge(slot_ready[s], 16 * (l * ROUNDS + 3))
                    for k in range(KD):
                        s, kk = k // 4, k % 4
                        lhs = H[:, k, t * P:(t + 1) * P]
                        mm(PS[:, b0, :], lhs, ring[:, s, kk, 0:512], start=(k == 0), stop=(k == KD - 1))
                        mm(PS[:, b0 + 1, :], lhs, ring[:, 2 + s, kk, 256:768], start=(k == 0), stop=(k == KD - 1))
                        last = mm(PS[:, b0 + 2, 0:256], lhs, ring[:, 2 + s, kk, 768:1024],
                                  start=(k == 0), stop=(k == KD - 1))
                    last.then_inc(p_mm, 1)

                def step_q(l, t):
                    pe.wait_ge(ra_done, NT * l + t + 1)
                    if t < LT:
                        pe.wait_ge(rd_done, LT * l + t + 1)
                    else:
                        pe.wait_ge(p_ds, NT * l + t + 1)
                    banks01(l)
                    st = stage[:, t % 2, :]
                    for c in range(7):
                        last = tr(PS[:, c // 4, (c % 4) * P:(c % 4 + 1) * P], st[:, c * P:(c + 1) * P],
                                  ident[:, :])
                    last.then_inc(q_T, 1)

                def step_f(l, n):
                    if n < 2:
                        pe.wait_ge(p_v, NT * l + LT + n)
                        pe.wait_ge(p_qs, NT * l + LT + n)
                    if n >= 3:
                        pe.wait_ge(f_act, 4 * l + n - 2)
                    s0, c0 = FCHUNK[n]
                    for k in range(KD):
                        lhs = ring[:, s0 + k // 4, k % 4, c0:c0 + P]
                        mm(PS[:, 2 + 2 * ((n + 2) % 3), :], lhs, H[:, k, 0:LAT], start=(k == 0), stop=(k == KD - 1))
                        last = mm(PS[:, 3 + 2 * ((n + 2) % 3), 0:CTX], lhs, H[:, k, LAT:TOK],
                                  start=(k == 0), stop=(k == KD - 1))
                    last.then_inc(f_mm, 1)

                for kind, n in ORDER:
                    if kind == "x":
                        step_x(l, n)
                    elif kind == "j":
                        step_j(l, n)
                    elif kind == "q":
                        step_q(l, n)
                    elif kind == "f":
                        step_f(l, n)
                pe.wait_ge(f_mm, 6 * l + 6)
                for s in range(4):
                    pe.nop().then_inc(slot_used[s], 1)
                finish_phase(l, 2)

                def scores(l, n):
                    t, gqa, h, m = score_map(n)
                    if n >= 2:
                        pe.wait_ge(t_exp, NM * l + n - 1)
                    b0 = 2 * (n % 2)
                    if n % 4 == 0:
                        pe.wait_ge(q_spread, SPREADS * l + n // 4 + 1)
                    kc, cc = (2, 0) if gqa else (5 + h // 2, 1 + h // 2)
                    lhs = spread_queries(n // 4)[:, n % 4, :]
                    if t < LT:
                        mm(PS[:, b0, :], lhs, qkT[:, kc, 0:LAT], start=True, stop=True)
                        last = mm(PS[:, b0 + 1, 0:P], lhs, kcT[:, cc, :], start=True, stop=True)
                    else:
                        last = mm(PS[:, b0, 0:P], lhs, qkT[:, kc, LAT:TOK], start=True, stop=True)
                    last.then_inc(t_scores, 1)

                def turn_probs(l, n):
                    t = n // MAPS
                    pe.wait_ge(t_exp, NM * l + n + 1)
                    if n >= 1:
                        pe.wait_ge(t_pt, NM * l + n)
                    if n > OUT_AT:
                        pe.wait_ge(t_oTe, NT * l + (n - OUT_AT - 1) // MAPS + 1)
                    for c in range(LT + 1 if t < LT else 1):
                        last = tr(PS[:, 4 + c // 4, (c % 4) * P:(c % 4 + 1) * P],
                                  Pm[:, n % 3, c * P:(c + 1) * P], ident[:, :])
                    last.then_inc(t_pT, 1)

                def values(l, n):
                    t, gqa, h, m = score_map(n)
                    if n % MAPS == 0 and t >= 1:
                        pe.wait_ge(t_taken, NT * l + t)
                    pe.wait_ge(t_pt, NM * l + n + 1)
                    chunks = LT + 1 if t < LT else 1
                    o0 = HD * out_slot(n)
                    for c in range(chunks):
                        if c == LT:
                            v = cv[:, HD * (h // 2):HD * (h // 2 + 1)] if gqa else cv[:, P + HD * h:P + HD * (h + 1)]
                        else:
                            kt = c if t < LT else LT
                            v = vA[:, kt, HD * (h // 2):HD * (h // 2 + 1)] if gqa else vD[:, kt, HD * h:HD * (h + 1)]
                        last = mm(PS[:, 6 + o0 // 512, o0 % 512:o0 % 512 + HD], PT[:, n % 2, c * P:(c + 1) * P], v,
                                  start=(c == 0), stop=(c == chunks - 1))
                    last.then_inc(t_pv, 1)

                def turn_out(l, t, n):
                    pe.wait_ge(t_otok, NT * l + t + 1)
                    pe.wait_ge(t_pt, NM * l + min(n + 1, NM))
                    for c in range(4):
                        last = tr(PS[:, 4, c * P:(c + 1) * P], o_tok[:, c * P:(c + 1) * P], ident[:, :])
                    last.then_inc(t_oT, 1)

                scores(l, 0)
                scores(l, 1)
                for n in range(NM + 4):
                    if n + 2 < NM:
                        scores(l, n + 2)
                    if n < NM:
                        turn_probs(l, n)
                    if 1 <= n <= NM:
                        values(l, n - 1)
                    if n >= OUT_AT and (n - OUT_AT) % MAPS == 0:
                        turn_out(l, (n - OUT_AT) // MAPS, n)
                finish_phase(l, 3)

                def project_out(l, t, chunks=(0, 1, 6, 7, 2, 3, 4, 5)):
                    if t >= 2:
                        pe.wait_ge(o_g, NT * l + t - 1)
                    for k in chunks:
                        for c in range(2):
                            last = mm(PS[:, 2 * (t % 2) + c, :], H[:, k, t * P:(t + 1) * P],
                                      ring[:, 4 + k // 4, k % 4, c * 512:(c + 1) * 512],
                                      start=(k == 0), stop=(k == 5))
                    if k == 5:
                        last.then_inc(o_mm, 1)

                def mix_pools(i):
                    mm(PS[:, 2 * i, :], pool_w[:, i, :], poolD3[:, i, 0:LAT], start=True, stop=True)
                    mm(PS[:, 2 * i + 1, 0:CTX], pool_w[:, i, :], poolD3[:, i, CTX0 - PAD:OUTW],
                       start=True, stop=True).then_inc(c_mix, 1)

                def channel_mean(b, src, done):
                    for i in range(2):
                        mm(PS[:, b, :], mean_w[:, :], src[:, i, 0:512], start=(i == 0), stop=(i == 1))
                        last = mm(PS[:, b + 1, 0:OUTW - 512], mean_w[:, :], src[:, i, 512:OUTW],
                                  start=(i == 0), stop=(i == 1))
                    last.then_inc(done, 1)

                pe.wait_ge(c_y, l + 1)
                channel_mean(4, y3, c_mean)
                mix_pools(0)
                pe.wait_ge(c_sq, 2 * l + 2)
                channel_mean(6, ysq, c_var)
                mix_pools(1)
                pe.wait_ge(c_mixe, 4 * l + 1)
                for s in (4, 5):
                    pe.wait_ge(slot_ready[s], 16 * (l * ROUNDS + 3))
                project_out(l, 0, (0, 1, 6, 7))
                pe.wait_ge(c_z, 2 * l + 2)
                for co in range(2):
                    for ci in range(2):
                        lhs = conv_pw[:, ci, co * P:(co + 1) * P]
                        mm(PS[:, 4 + 2 * co, :], lhs, y3[:, ci, 0:LAT], start=(ci == 0), stop=(ci == 1))
                        last = mm(PS[:, 5 + 2 * co, 0:CTX], lhs, y3[:, ci, CTX0 - PAD:OUTW],
                                  start=(ci == 0), stop=(ci == 1))
                    last.then_inc(c_pw, 1)
                finish_phase(l, 4)

                def norm2_turn(l, t):
                    pe.wait_ge(o_xn, NT * l + t + 1)
                    if t >= 1:
                        pe.wait_ge(o_h4, NT * l + t)
                        pe.wait_ge(o_h5, NT * l + t)
                    for j in range(KD):
                        last = tr(PS[:, 4 + j // 4, (j % 4) * P:(j % 4 + 1) * P],
                                  xnb[:, t % 2, j * P:(j + 1) * P], ident[:, :])
                    last.then_inc(o_xT, 1)

                def route(l, t):
                    pe.wait_ge(o_h4, NT * l + t + 1)
                    pe.wait_ge(o_h5, NT * l + t + 1)
                    for k in range(KD):
                        last = mm(PS[:, 6, t * EXPERTS:(t + 1) * EXPERTS], H[:, k, t * P:(t + 1) * P],
                                  router[:, k, :], start=(k == 0), stop=(k == KD - 1))
                    last.then_inc(o_lg, 1)

                project_out(l, 0, (2, 3, 4, 5))
                for t in range(NT):
                    if t + 1 < NT:
                        project_out(l, t + 1)
                    if t >= 1:
                        route(l, t - 1)
                    norm2_turn(l, t)
                route(l, LT)
                pe.wait_ge(o_mm, NT * l + NT)
                for s in (4, 5):
                    pe.nop().then_inc(slot_used[s], 1)
                pe.wait_ge(r_aff, l + 1)
                for t in range(NT):
                    dst = PS[0:EXPERTS, 7, t * P:(t + 1) * P] if t < LT else PS[0:EXPERTS, 6, P:2 * P]
                    last = tr(dst, aff[:, t * EXPERTS:(t + 1) * EXPERTS], ident[:, :])
                last.then_inc(r_affT, 1)
                wait_apart(pe, k_top, l + 1)
                tr(PS[0:CAP, 0, 0:EXPERTS], topf[0:EXPERTS, :], ident[0:EXPERTS, 0:EXPERTS])
                tr(PS[0:CAP, 0, 16:16 + EXPERTS], topv[0:EXPERTS, :],
                   ident[0:EXPERTS, 0:EXPERTS]).then_inc(k_T, 1)
                finish_phase(l, 5)

                def turn_rows(part, xp, done):
                    for j in range(4):
                        jj = 4 * part + j
                        last = tr(PS[:, 6 + part, j * CAP:(j + 1) * CAP], xg[0:CAP, xp, jj * P:(jj + 1) * P],
                                  ident[0:CAP, 0:CAP])
                    last.then_inc(done, 1)

                def expert(l, e, e2, p):
                    done = l * EXPERTS + e
                    rnd = l * ROUNDS + 3 + e
                    pe.wait_ge(e_xe, 17 * l + e + 1)
                    pe.wait_ge(e_sil, 2 * done + CREDIT)
                    for h in range(2):
                        pe.wait_ge(slot_ready[h], 16 * (rnd + 1))
                        for kk in range(4):
                            k = 4 * h + kk
                            for c in range(2):
                                last = mm(PS[0:CAP, c, :], xeT[:, k, :], ring[:, h, kk, c * 512:(c + 1) * 512],
                                          start=(k == 0), stop=(k == KD - 1))
                        last.then_inc(slot_used[h], 1)
                    def turn_hidden(part, done_sem):
                        pe.wait_ge(e_hid, 2 * done + 1 + part + CREDIT)
                        for j in range(4):
                            jj = 4 * part + j
                            last = tr(PS[:, 6 + part, j * CAP:(j + 1) * CAP], hid[0:CAP, jj * P:(jj + 1) * P],
                                      ident[0:CAP, 0:CAP])
                        last.then_inc(done_sem, 1)

                    pe.wait_ge(e_hid, 2 * done + CREDIT)
                    for h in range(2):
                        pe.wait_ge(slot_ready[2 + h], 16 * (rnd + 1))
                    for c in range(2):
                        for k in range(KD):
                            last = mm(PS[0:CAP, 2 + c, :], xeT[:, k, :],
                                      ring[:, 2 + k // 4, k % 4, c * 512:(c + 1) * 512],
                                      start=(k == 0), stop=(k == KD - 1))
                            if c == 1 and k % 4 == 3:
                                last.then_inc(slot_used[2 + k // 4], 1)
                            if c == 1 and k == KD - 3:
                                turn_hidden(0, e_T0)
                        if c == 0:
                            last.then_inc(e_U0, 1)

                    def down(k):
                        for c in range(2):
                            last = mm(PS[0:CAP, 4 + c, :], hidT[:, k, :],
                                      ring[:, 4 + k // 4, k % 4, c * 512:(c + 1) * 512],
                                      start=(k == 0), stop=(k == KD - 1))
                        if k % 4 == 3:
                            last.then_inc(slot_used[4 + k // 4], 1)

                    pe.wait_ge(e_hT0, done + 1)
                    pe.wait_ge(e_y, done + CREDIT)
                    pe.wait_ge(slot_ready[4], 16 * (rnd + 1))
                    for k in range(3):
                        down(k)
                    turn_hidden(1, e_T1)
                    down(3)
                    pe.wait_ge(e_gath[1 - p], 16 * (l * (8 + p) + e2 + 1))
                    turn_rows(0, 1 - p, e_X0)
                    pe.wait_ge(e_hT1, done + 1)
                    pe.wait_ge(slot_ready[5], 16 * (rnd + 1))
                    down(4)
                    down(5)
                    turn_rows(1, 1 - p, e_X1)
                    down(6)
                    down(7)

                pe.wait_ge(e_gath[0], 16 * (9 * l + 1))
                turn_rows(0, 0, e_X0)
                turn_rows(1, 0, e_X1)
                with pe.Fori(0, EXPERTS // 2) as e2:
                    expert(l, 2 * e2, e2, 0)
                    expert(l, 2 * e2 + 1, e2 + 1, 1)
                finish_phase(l, 6)

        @block.scalar
        def _(act):
            do = nc.scalar.activation
            act.sem_inc(e_sil, CREDIT)

            def finish_phase(l, k):
                act.drain().then_inc(phase_done, 1)
                act.wait_ge(phase_done, 4 * (l * PHASES + k))

            act.dma_start(x_dram[0:LAT, :], ins["x_sample"][0, :, :]).then_inc(x_seeded, 16)
            act.dma_start(x_dram[LAT:TOK, :], ins["x_prompt"][0, :, :]).then_inc(x_seeded, 16)
            act.wait_ge(c_turned, 1)
            act.wait_ge(consts_set, 3)
            do(scT[:, :, 0:2], PS[:, 7, 0:16].rearrange("p (v j) -> p j v", v=2), ACT.Silu).then_inc(silu_c, 1)
            act.wait_ge(x_seeded, 32)

            with act.Fori(0, LAYERS) as l:
                def load(dst, src):
                    act.dma_start(dst, src).then_inc(params_loaded, 16)

                load(prow[24:72, :], ins["b_mod"][l, :].rearrange("(j p) -> j p", p=P))
                for r0, name, n in ((0, "norm1_g", 8), (8, "norm2_g", 8), (16, "pool_scale", 2),
                                    (18, "conv_dw_b", 2), (20, "conv_ln_g", 2), (22, "conv_ln_b", 2)):
                    load(prow[r0:r0 + n, :], ins[name][l, :].rearrange("(j p) -> j p", p=P))
                load(cwrow, ins["conv_dw_w"][l, :, :])
                for i, name in enumerate(("gqa_qn_g", "gqa_kn_g", "diff_subln_g")):
                    load(head_g[:, i, :], ins[name][bass.ds(l, 1), :].to_broadcast([P, HD]))
                for i, name in enumerate(("diff_lq1", "diff_lk1", "diff_lq2", "diff_lk2")):
                    load(lamv[:, i, :], ins[name][bass.ds(l, 1), :].to_broadcast([P, 32]))
                load(lamc[:, :], ins["k_lam"][bass.ds(l, 1), :].to_broadcast([P, 2]))
                load(router[:, :, :], ins["router_w"][l, :, :].rearrange("(k p) e -> p k e", p=P))
                for g in range(4):
                    r0 = HD * (g % 2)
                    load(pool_w[r0:r0 + HD, g // 2, r0:r0 + HD], ins["pool_w"][l, g, :, :])
                load(conv_pw[:, :, :], ins["conv_pw_w"][l, :, :].rearrange("(i p) n -> p i n", p=P))
                load(ck[:, 0:P], ins["cache_gqa_k"][0, l, :, :, :].rearrange("t h d -> t (h d)"))
                load(ck[:, P:384], ins["cache_diff_k"][0, l, :, :, :].rearrange("t h d -> t (h d)"))
                load(cv[:, 0:P], ins["cache_gqa_v"][0, l, :, :, :].rearrange("t h d -> t (h d)"))
                load(cv[:, P:384], ins["cache_diff_v"][0, l, :, :, :].rearrange("t h d -> t (h d)"))
                def load_x(l, t):
                    if t >= 2:
                        act.wait_ge(n_xT, NT * l + t - 1)
                    act.dma_start(xt[t % 2], x_dram[t * P:(t + 1) * P, :]).then_inc(x_loaded[t % 2], 16)

                load_x(l, 0)
                load_x(l, 1)
                act.wait_ge(lam_sums, l + 1)
                do(lams[:, 2:4], lams[:, 0:2], ACT.Exp).then_inc(lam_exps, 1)
                act.wait_ge(kc_turned, l + 1)
                do(kcT[:, :, :].rearrange("p i n -> p (i n)"), PS[:, 7, 0:384], ACT.Copy)
                act.wait_ge(gates_turned, l + 1)
                do(gate_rows[:, :], PS[0:32, 0, 0:P], ACT.Copy).then_inc(gates_taken, 1)
                act.wait_ge(gates_taken, l + 1)
                act.dma_start(modg.rearrange("v i (j p) -> (v i j) p", p=P), gate_rows[:, :]).then_inc(gates_saved, 16)
                finish_phase(l, 1)

                def squares(l, t):
                    act.wait_ge(x_loaded[t % 2], 16 * parity_count(l, t))
                    if t >= 1:
                        act.wait_ge(n_ss, NT * l + t)
                    do(junk, xt[t % 2], ACT.Square, accum_out=stat[:, t:t + 1]).then_inc(n_ss, 1)

                def step_x(l, t):
                    act.wait_ge(n_xT, NT * l + t + 1)
                    v = 0 if t < LT else 1
                    for j in range(4):
                        last = do(H[:, j, t * P:(t + 1) * P], PS[:, 0, j * P:(j + 1) * P], ACT.Identity,
                                  bias=modB[:, 0, v, j:j + 1], scale=modA[:, 0, v, j:j + 1])
                    last.then_inc(b0_evac, 1)

                def step_j(l, t):
                    b0 = 2 + 3 * (t % 2)
                    act.wait_ge(p_mm, NT * l + t + 1)
                    if t >= 1:
                        act.wait_ge(p_ms, NT * l + t)
                    do(vA[:, t, :], PS[:, b0, 384:512], ACT.Copy)
                    do(qsq, PS[:, b0, 0:384], ACT.Square).then_inc(p_sq, 1)
                    if t >= 2:
                        act.wait_ge(q_T, NT * l + t - 1)
                    do(stage[:, t % 2, 384:896], PS[:, b0 + 1, :], ACT.Copy).then_inc(p_ds, 1)
                    do(vD[:, t, :], PS[:, b0 + 2, 0:256], ACT.Copy).then_inc(p_v, 1)

                def step_q(l, t):
                    act.wait_ge(q_T, NT * l + t + 1)
                    do(qkT[:, 0:4, t * P:(t + 1) * P], PS[:, 0, :].rearrange("p (c n) -> p c n", c=4),
                       ACT.Copy).then_inc(b0_evac, 1)

                def step_f(l, n):
                    if n in (3, 5):
                        return
                    src = pair(2 + 2 * ((n + 2) % 3), TOK)
                    act.wait_ge(f_mm, 6 * l + n + 1)
                    if n < 2:
                        do(poolT[:, n, PAD:PAD + LAT], src[:, 0:LAT], ACT.Copy)
                        do(poolT[:, n, CTX0:CTX0 + CTX], src[:, LAT:TOK], ACT.Copy).then_inc(f_act, 1)
                    else:
                        if n == 4:
                            act.wait_ge(f_u, 2 * l + 1)
                        do(sig, src, ACT.Sigmoid).then_inc(f_act, 1)

                squares(l, 0)
                squares(l, 1)
                for kind, n in TAKE_ORDER:
                    if kind == "x":
                        step_x(l, n)
                        if n + 2 < NT:
                            load_x(l, n + 2)
                    elif kind == "s":
                        squares(l, n)
                    elif kind == "j":
                        step_j(l, n)
                    elif kind == "q":
                        step_q(l, n)
                    elif kind == "f":
                        step_f(l, n)
                act.wait_ge(p_v, NT * l + NT)
                act.wait_ge(ra_done, NT * l + NT)
                for name, src in (("state_gqa_k", stage[:, 0, 256:384]), ("state_gqa_v", vA[:, LT, :]),
                                  ("state_diff_k", stage[:, 0, 640:896]), ("state_diff_v", vD[:, LT, :])):
                    act.dma_start(outs[name][0, l, :, :, :].rearrange("t h d -> t (h d)"), src)\
                       .then_inc(state_saved, 16)
                finish_phase(l, 2)

                def exponentials(l, n):
                    t, gqa, h, m = score_map(n)
                    act.wait_ge(t_max, NM * l + n + 1)
                    if n >= 3:
                        act.wait_ge(t_pT, NM * l + n - 2)
                    w = TOK if t < LT else P
                    r = 64 + 12 * (t % 2) + out_slot(n)
                    do(Pm[:, n % 3, 0:w], pair(2 * (n % 2), w), ACT.Exp, bias=stat[:, 8 + n % 4:9 + n % 4],
                       scale=(HD ** -0.5 if gqa else 32 ** -0.5), accum_out=stat[:, r:r + 1]).then_inc(t_exp, 1)

                def take_probs(l, n):
                    act.wait_ge(t_pT, NM * l + n + 1)
                    if n >= 2:
                        act.wait_ge(t_pv, NM * l + n - 1)
                    w = TOK if n // MAPS < LT else P
                    do(PT[:, n % 2, 0:w], pair(4, w), ACT.Copy).then_inc(t_pt, 1)

                def take_out(l, t):
                    act.wait_ge(t_oT, NT * l + t + 1)
                    src = PS[:, 4, :].rearrange("p (c n) -> p c n", c=4)
                    do(H[:, 0:2, t * P:(t + 1) * P], src[:, 0:2, :], ACT.Copy)
                    do(H[:, 6:8, t * P:(t + 1) * P], src[:, 2:4, :], ACT.Copy).then_inc(t_oTe, 1)

                exponentials(l, 0)
                for n in range(NM + 4):
                    if n + 1 < NM:
                        exponentials(l, n + 1)
                    if n < NM:
                        take_probs(l, n)
                    if n >= OUT_AT and (n - OUT_AT) % MAPS == 0:
                        take_out(l, (n - OUT_AT) // MAPS)
                wait_apart(act, state_saved, 64 * (l + 1))
                finish_phase(l, 3)

                def take_mix(i, src, chunk, done, scale=1.0):
                    do(H[:, chunk, :], src, ACT.Copy, scale=scale).then_inc(done, 1)

                def take_pool(l, i):
                    act.wait_ge(c_mix, 2 * l + i + 1)
                    take_mix(i, pair(2 * i, TOK), 2 + i, c_mixe, scale=pT[:, 16 + i:17 + i])

                for i in range(2):
                    act.wait_ge(c_yc, 2 * l + i + 1)
                    do(ysq[:, i, :], y3[:, i, :], ACT.Square).then_inc(c_sq, 1)
                take_pool(l, 0)
                act.wait_ge(c_vs, l + 1)
                do(rstd_y, rstd_y, ACT.Sqrt).then_inc(c_rs, 1)
                take_pool(l, 1)
                for i in range(2):
                    act.wait_ge(c_yn, 2 * l + i + 1)
                    do(y3[:, i, :], y3[:, i, :], ACT.Silu, bias=pT[:, 22 + i:23 + i],
                       scale=pT[:, 20 + i:21 + i]).then_inc(c_z, 1)
                for i in range(2):
                    act.wait_ge(c_pw, 2 * l + i + 1)
                    take_mix(i, pair(4 + 2 * i, TOK), 4 + i, c_mixe)
                finish_phase(l, 4)

                wait_apart(act, gates_saved, 16 * (l + 1))
                for v in range(2):
                    act.dma_start(gb1[:, v, :], modg[v:v + 1, 0, :].to_broadcast([P, D])).then_inc(g_loaded, 16)
                act.dma_start(g2b[0:CAPL, :], modg[0:1, 1, :].to_broadcast([CAPL, D])).then_inc(g_loaded, 16)
                act.dma_start(g2b[CAPL:CAP, :], modg[1:2, 1, :].to_broadcast([CAPC, D])).then_inc(g_loaded, 16)

                def load_xo(l, t):
                    if t >= 2:
                        act.wait_ge(x_saved[t % 2], 32 * parity_count(l, t - 2))
                    act.dma_start(xo[:, t % 2, :], x_dram[t * P:(t + 1) * P, :]).then_inc(xo_loaded[t % 2], 16)

                load_xo(l, 0)
                load_xo(l, 1)
                for t in range(NT):
                    act.wait_ge(o_x, NT * l + t + 1)
                    if t >= 1:
                        act.wait_ge(o_ss, NT * l + t)
                    do(junk2, xo[:, t % 2, :], ACT.Square, accum_out=stat[:, 16 + t:17 + t]).then_inc(o_ss, 1)
                    act.dma_start(x_dram[t * P:(t + 1) * P, :], xo[:, t % 2, :]).then_inc(x_saved[t % 2], 16)
                    act.wait_ge(o_xn, NT * l + t + 1)
                    act.dma_start(xn_dram[t * P:(t + 1) * P, :], xnb[:, t % 2, :]).then_inc(x_saved[t % 2], 16)
                    act.wait_ge(o_xT, NT * l + t + 1)
                    v = 0 if t < LT else 1
                    for j in range(4):
                        last = do(H[:, j, t * P:(t + 1) * P], PS[:, 4, j * P:(j + 1) * P], ACT.Identity,
                                  bias=modB[:, 1, v, j:j + 1], scale=modA[:, 1, v, j:j + 1])
                    last.then_inc(o_h4, 1)
                    if t + 2 < NT:
                        load_xo(l, t + 2)
                act.wait_ge(r_sub, l + 1)
                do(logit, logit, ACT.Exp).then_inc(r_exp, 1)
                act.wait_ge(r_affT, l + 1)
                do(affT[0:EXPERTS, 0:LAT], PS[0:EXPERTS, 7, :], ACT.Copy)
                do(affT[0:EXPERTS, LAT:TOK], PS[0:EXPERTS, 6, P:2 * P], ACT.Copy).then_inc(r_affs, 1)
                for p in range(2):
                    wait_apart(act, x_saved[p], 32 * X_LOADS[p] * (l + 1))
                finish_phase(l, 5)

                def take_rows(l, n):
                    for part, turned in ((0, e_X0), (1, e_X1)):
                        act.wait_ge(turned, 17 * l + n + 1)
                        for j in range(4):
                            jj = 4 * part + j
                            for v, c0, c1 in ((0, 0, CAPL), (1, CAPL, CAP)):
                                last = do(xeT[:, jj, c0:c1], PS[:, 6 + part, j * CAP + c0:j * CAP + c1],
                                          ACT.Identity, bias=modB[:, 1, v, jj:jj + 1],
                                          scale=modA[:, 1, v, jj:jj + 1])
                    last.then_inc(e_xe, 1)

                take_rows(l, 0)
                with act.Fori(0, EXPERTS) as e:
                    done = l * EXPERTS + e
                    act.wait_ge(slot_used[1], l * ROUNDS + 4 + e + CREDIT)
                    act.wait_ge(e_hid, 2 * done + CREDIT)
                    for c in range(2):
                        do(sil[0:CAP, c * 512:(c + 1) * 512], PS[0:CAP, c, :], ACT.Silu).then_inc(e_sil, 1)
                    take_rows(l, e + 1)
                finish_phase(l, 6)

            for t in range(NT):
                act.dma_start(xf[:, t, :], x_dram[t * P:(t + 1) * P, :]).then_inc(fin_x[t], 16)
            for t in range(NT):
                act.wait_ge(fin_x[t], 16)
                if t >= 1:
                    act.wait_ge(fin_ss, t)
                do(junk2, xf[:, t, :], ACT.Square, accum_out=stat[:, 16 + t:17 + t]).then_inc(fin_ss, 1)

        @block.vector
        def _(dve):
            V = nc.vector
            dve.sem_inc(e_hid, CREDIT)
            dve.sem_inc(e_y, CREDIT)
            chain = [0, 0]

            def link(ins_, bare=False):
                chain[0] += 1
                ins_.then_inc(tensor_chain, 1)
                if bare:
                    wait_apart(dve, tensor_chain, chain[1] + chain[0])
                else:
                    dve.wait_ge(tensor_chain, chain[1] + chain[0])

            def finish_phase(l, k):
                dve.drain().then_inc(phase_done, 1)
                dve.wait_ge(phase_done, 4 * (l * PHASES + k))

            def heads(ap, n):
                return ap.rearrange("p (h d) -> p h d", h=n)

            with dve.Fori(0, LAYERS) as l:
                chain[0], chain[1] = 0, l * V_LINKS
                def take_mod(l, b):
                    rnd, m = divmod(b, 3)
                    dve.wait_ge(slot_used[2 * m + 1], l * ROUNDS + rnd + 1 + CREDIT)
                    V.tensor_copy(modrow[:, b, :], PS[:, b % 3, 0:256]).then_inc(mod_taken, 1)

                for b in range(5):
                    take_mod(l, b)
                dve.wait_ge(params_loaded, 16 * N_PARAMS * (l + 1))
                link(V.tensor_tensor(lamw[:, :, :], lamv[:, 0:4:2, :], lamv[:, 1:4:2, :], ALU.mult))
                V.tensor_reduce(lams[:, 0:2], lamw[:, :, :], AX.X, ALU.add).then_inc(lam_sums, 1)
                V.tensor_scalar(subg[:, :], head_g[:, 2, :], lamc[:, 1:2], None, ALU.mult)
                dve.wait_ge(lam_exps, l + 1)
                link(V.tensor_tensor(lams[:, 4:5], lams[:, 3:4], lams[:, 2:3], ALU.subtract))
                V.tensor_scalar(lams[:, 5:6], lams[:, 4:5], lamc[:, 0:1], None, ALU.subtract)
                dve.wait_ge(params_turned, l + 1)
                V.tensor_copy(cwT[:, :, 0:TAPS],
                              PS[:, 3, 96:160].rearrange("p (i n) -> p i n", i=2)[:, :, 0:TAPS])
                link(V.tensor_copy(pT[:, :], PS[:, 3, 0:72]))
                take_mod(l, 5)
                dve.wait_ge(mod_turned, 6 * l + 6)
                for b in range(6):
                    turned = PS[:, 4 + b // 2, 256 * (b % 2):256 * (b % 2) + 256]
                    last = V.tensor_tensor(mod[:, b, :, :].rearrange("p (q i) v -> p i q v", i=2),
                                           turned.rearrange("p (i q w) -> p i q w", i=2, q=4)[:, :, :, 0:2],
                                           pT[:, 24 + KD * b:24 + KD * (b + 1)].rearrange("p (q i) -> p i q", i=2)
                                           .unsqueeze(3).to_broadcast([P, 2, 4, 2]), ALU.add)
                link(last)
                for i, b in enumerate((2, 5)):
                    last = V.tensor_copy(gate_cols.rearrange("p (v i j) -> p v i j", v=2, i=2)[:, :, i, :],
                                         mod[:, b, :, :].rearrange("p j v -> p v j"))
                last.then_inc(gates_picked, 1)
                for n in range(2):
                    V.tensor_copy(modB[:, n, :, :], mod[:, 3 * n, :, :].rearrange("p j v -> p v j"))
                    for v in range(2):
                        V.scalar_tensor_tensor(modA[:, n, v, :], mod[:, 3 * n + 1, :, v], 1.0,
                                               pT[:, KD * n:KD * (n + 1)], ALU.add, ALU.mult)
                finish_phase(l, 1)

                def normalise(l, t):
                    dve.wait_ge(n_rstd, NT * l + t + 1)
                    V.tensor_scalar(xt[t % 2], xt[t % 2], stat[:, 24 + t:25 + t], None, ALU.mult).then_inc(n_xn, 1)

                def step_x(l, t):
                    dve.wait_ge(n_xT, NT * l + t + 1)
                    v = 0 if t < LT else 1
                    for j in range(4):
                        last = V.tensor_scalar(H[:, 4 + j, t * P:(t + 1) * P], PS[:, 1, j * P:(j + 1) * P],
                                               modA[:, 0, v, 4 + j:5 + j], modB[:, 0, v, 4 + j:5 + j],
                                               ALU.mult, ALU.add)
                    last.then_inc(b1_evac, 1)

                def step_j(l, t):
                    b0 = 2 + 3 * (t % 2)
                    st = stage[:, t % 2, 0:384]
                    dve.wait_ge(p_sq, NT * l + t + 1)
                    V.tensor_reduce(stat[:, 32:38], heads(qsq, 6), AX.X, ALU.add).then_inc(p_ms, 1)
                    dve.wait_ge(p_r, NT * l + t + 1)
                    if t >= 2:
                        dve.wait_ge(q_T, NT * l + t - 1)
                    V.tensor_tensor(st[:, 0:256].rearrange("p (c g d) -> p g c d", c=2, g=2),
                                    PS[:, b0, 0:256].rearrange("p (g c d) -> p g c d", c=2, g=2),
                                    stat[:, 38:42].rearrange("p (g c) -> p g c", g=2).unsqueeze(3)
                                    .to_broadcast([P, 2, 2, HD]), ALU.mult)
                    V.tensor_tensor(heads(st[:, 256:384], 2), heads(PS[:, b0, 256:384], 2),
                                    stat[:, 42:44].unsqueeze(2).to_broadcast([P, 2, HD]),
                                    ALU.mult).then_inc(p_qs, 1)
                    dve.wait_ge(p_qs, NT * l + t + 1)
                    fin = None
                    for i, h0, h1 in ((0, 0, 4), (1, 4, 6)):
                        seg = heads(st[:, h0 * HD:h1 * HD], h1 - h0)
                        fin = V.tensor_tensor(seg, seg, head_g[:, i, :].unsqueeze(1).to_broadcast([P, h1 - h0, HD]),
                                              ALU.mult)
                    if t == LT:
                        fin.then_inc(ra_done, 1)
                        return
                    link(fin)
                    x4 = st.rearrange("p (h d two) -> p h d two", h=6, two=2)
                    s4 = ra2.rearrange("p (h d two) -> p h d two", h=6, two=2)
                    ts = rope_a[:, t, 1, :].rearrange("p (d two) -> p d two", two=2)
                    V.tensor_tensor(heads(ra1, 6), heads(st, 6),
                                    rope_a[:, t, 0, :].unsqueeze(1).to_broadcast([P, 6, HD]), ALU.mult)
                    for a in range(2):
                        fin = V.tensor_tensor(s4[:, :, :, a], x4[:, :, :, 1 - a],
                                              ts[:, :, a].unsqueeze(1).to_broadcast([P, 6, HD // 2]), ALU.mult)
                    link(fin)
                    V.tensor_tensor(st, ra1, ra2, ALU.add).then_inc(ra_done, 1)

                def step_q(l, t):
                    dve.wait_ge(q_T, NT * l + t + 1)
                    V.tensor_copy(qkT[:, 4:7, t * P:(t + 1) * P],
                                  PS[:, 1, 0:384].rearrange("p (c n) -> p c n", c=3)).then_inc(b1_evac, 1)

                def step_f(l, n):
                    if n not in (3, 5):
                        return
                    i = (n - 3) // 2
                    src = pair(2 + 2 * ((n + 2) % 3), TOK)
                    dve.wait_ge(f_mm, 6 * l + n + 1)
                    dve.wait_ge(f_act, 4 * l + 3 + i)
                    V.tensor_tensor(u[:, i, PAD:PAD + LAT], src[:, 0:LAT], sig[:, 0:LAT], ALU.mult)
                    V.tensor_tensor(u[:, i, CTX0:CTX0 + CTX], src[:, LAT:TOK], sig[:, LAT:TOK],
                                    ALU.mult).then_inc(f_u, 1)

                normalise(l, 0)
                normalise(l, 1)
                for kind, n in TAKE_ORDER:
                    if kind == "x":
                        step_x(l, n)
                    elif kind == "s":
                        normalise(l, n)
                    elif kind == "j":
                        step_j(l, n)
                    elif kind == "q":
                        step_q(l, n)
                    elif kind == "f":
                        step_f(l, n)
                finish_phase(l, 2)

                def maximum(l, n):
                    t, gqa, h, m = score_map(n)
                    w = TOK if t < LT else P
                    dve.wait_ge(t_scores, NM * l + n + 1)
                    link(V.reduce_max(stat[:, 44 + n % 2:45 + n % 2], pair(2 * (n % 2), w), AX.X))
                    if n >= 4:
                        dve.wait_ge(t_exp, NM * l + n - 3)
                    V.tensor_scalar(stat[:, 8 + n % 4:9 + n % 4], stat[:, 44 + n % 2:45 + n % 2],
                                    -(HD ** -0.5) if gqa else -(32 ** -0.5), None, ALU.mult).then_inc(t_max, 1)

                def take_heads(l, t):
                    sums = stat[:, 64 + 12 * (t % 2):76 + 12 * (t % 2)]
                    over = stat[:, 88:100]
                    dve.wait_ge(t_exp, NM * l + MAPS * (t + 1))
                    link(V.reciprocal(over, sums))
                    link(V.tensor_scalar(over[:, 8:12], over[:, 8:12], lams[:, 5:6], None, ALU.mult))
                    dve.wait_ge(t_pv, NM * l + MAPS * (t + 1))
                    V.tensor_tensor(heads(o_raw, 12), heads(pair(6, 768), 12),
                                    over.unsqueeze(2).to_broadcast([P, 12, HD]), ALU.mult).then_inc(t_taken, 1)
                    dve.wait_ge(t_taken, NT * l + t + 1)
                    link(V.tensor_tensor(o_raw[:, 256:512], o_raw[:, 256:512], o_raw[:, 512:768], ALU.add))
                    link(V.tensor_tensor(osq, o_raw[:, 256:512], o_raw[:, 256:512], ALU.mult))
                    V.tensor_reduce(stat[:, 52:56], heads(osq, 4), AX.X, ALU.add).then_inc(t_dss, 1)

                def sub_norm(l, t):
                    if t >= 1:
                        dve.wait_ge(t_oT, NT * l + t)
                    V.tensor_copy(o_tok[:, 0:256], o_raw[:, 0:256])
                    dve.wait_ge(t_dr, NT * l + t + 1)
                    link(V.tensor_tensor(heads(osq, 4), heads(o_raw[:, 256:512], 4),
                                         stat[:, 56:60].unsqueeze(2).to_broadcast([P, 4, HD]), ALU.mult))
                    V.tensor_tensor(heads(o_tok[:, 256:512], 4), heads(osq, 4),
                                    subg[:, :].unsqueeze(1).to_broadcast([P, 4, HD]), ALU.mult).then_inc(t_otok, 1)

                def conv_tap(i, k):
                    if k == 0:
                        link(V.tensor_scalar(y3[:, i, :], u[:, i, 0:OUTW], cwT[:, i, 0:1], pT[:, 18 + i:19 + i],
                                             ALU.mult, ALU.add))
                    else:
                        link(V.scalar_tensor_tensor(y3[:, i, :], u[:, i, k:k + OUTW], cwT[:, i, k:k + 1],
                                                    y3[:, i, :], ALU.mult, ALU.add))

                taps = [(0, k) for k in range(TAPS)] + [(1, k) for k in range(DVE_TAPS)]
                maximum(l, 0)
                maximum(l, 1)
                for n in range(NM + 4):
                    if n + 2 < NM:
                        maximum(l, n + 2)
                    if n >= MAPS and n % MAPS == 0:
                        take_heads(l, n // MAPS - 1)
                    elif n >= MAPS and n % MAPS == 1:
                        sub_norm(l, n // MAPS - 1)
                    elif taps:
                        conv_tap(*taps.pop(0))
                assert not taps
                finish_phase(l, 3)

                V.tensor_tensor(y3[:, 1, :], y3[:, 1, :], wb[:, 0:OUTW], ALU.add).then_inc(c_y, 1)
                dve.wait_ge(c_mean, l + 1)
                for i in range(2):
                    V.tensor_tensor(y3[:, i, :], y3[:, i, :], pair(4, OUTW), ALU.subtract).then_inc(c_yc, 1)
                dve.wait_ge(c_var, l + 1)
                V.tensor_scalar(rstd_y, pair(6, OUTW), EPS, None, ALU.add).then_inc(c_vs, 1)
                dve.wait_ge(c_rs, l + 1)
                link(V.reciprocal(rstd_y, rstd_y))
                for i in range(2):
                    V.tensor_tensor(y3[:, i, :], y3[:, i, :], rstd_y, ALU.mult).then_inc(c_yn, 1)
                finish_phase(l, 4)

                dve.wait_ge(g_loaded, 64 * (l + 1))

                def residual(l, t):
                    dve.wait_ge(o_mm, NT * l + t + 1)
                    V.tensor_tensor(gated, pair(2 * (t % 2)), gb1[:, 0 if t < LT else 1, :],
                                    ALU.mult).then_inc(o_g, 1)
                    dve.wait_ge(o_g, NT * l + t + 1)
                    dve.wait_ge(xo_loaded[t % 2], 16 * parity_count(l, t))
                    V.tensor_tensor(xo[:, t % 2, :], xo[:, t % 2, :], gated, ALU.add).then_inc(o_x, 1)

                residual(l, 0)
                for t in range(NT):
                    dve.wait_ge(o_r, NT * l + t + 1)
                    if t >= 2:
                        dve.wait_ge(o_xT, NT * l + t - 1)
                        dve.wait_ge(x_saved[t % 2], 32 * parity_count(l, t - 2))
                    V.tensor_scalar(xnb[:, t % 2, :], xo[:, t % 2, :], stat[:, 24 + t:25 + t], None,
                                    ALU.mult).then_inc(o_xn, 1)
                    dve.wait_ge(o_xT, NT * l + t + 1)
                    v = 0 if t < LT else 1
                    for j in range(4):
                        last = V.tensor_scalar(H[:, 4 + j, t * P:(t + 1) * P], PS[:, 5, j * P:(j + 1) * P],
                                               modA[:, 1, v, 4 + j:5 + j], modB[:, 1, v, 4 + j:5 + j],
                                               ALU.mult, ALU.add)
                    last.then_inc(o_h5, 1)
                    if t + 1 < NT:
                        residual(l, t + 1)
                dve.wait_ge(o_lg, NT * (l + 1))
                lg3 = PS[:, 6, 0:80].rearrange("p (t e) -> p t e", t=NT)
                link(V.reduce_max(stat[:, 32:37], lg3, AX.X))
                V.tensor_tensor(logit.rearrange("p (t e) -> p t e", t=NT), lg3,
                                stat[:, 32:37].unsqueeze(2).to_broadcast([P, NT, EXPERTS]),
                                ALU.subtract).then_inc(r_sub, 1)
                dve.wait_ge(r_exp, l + 1)
                link(V.tensor_reduce(stat[:, 38:43], logit.rearrange("p (t e) -> p t e", t=NT), AX.X, ALU.add))
                link(V.reciprocal(stat[:, 32:37], stat[:, 38:43]))
                V.tensor_tensor(aff.rearrange("p (t e) -> p t e", t=NT), logit.rearrange("p (t e) -> p t e", t=NT),
                                stat[:, 32:37].unsqueeze(2).to_broadcast([P, NT, EXPERTS]),
                                ALU.mult).then_inc(r_aff, 1)
                wait_apart(dve, r_affs, l + 1)
                for lo, hi, s0, n in ((0, LAT, 0, CAPL), (LAT, TOK, CAPL, CAPC)):
                    row = affT[0:EXPERTS, lo:hi]
                    for i in range(n // 8):
                        s = slice(s0 + 8 * i, s0 + 8 * i + 8)
                        link(V.max(topv[0:EXPERTS, s], row), bare=True)
                        V.max_index(topi[0:EXPERTS, s], topv[0:EXPERTS, s], row)
                        link(V.match_replace(row, topv[0:EXPERTS, s], row, -1.0), bare=True)
                link(V.tensor_copy(topf[0:EXPERTS, :], topi[0:EXPERTS, :]))
                V.tensor_scalar(topf[0:EXPERTS, CAPL:CAP], topf[0:EXPERTS, CAPL:CAP], float(LAT), None,
                                ALU.add).then_inc(k_top, 1)
                dve.wait_ge(k_T, l + 1)
                V.tensor_copy(idxT[0:CAP, 0:EXPERTS], PS[0:CAP, 0, 0:EXPERTS])
                V.tensor_copy(idxT[0:CAP, EXPERTS:EXPERTS + 1], PS[0:CAP, 0, 0:1])
                V.tensor_copy(gateT[0:CAP, 0:EXPERTS], PS[0:CAP, 0, 16:16 + EXPERTS])
                finish_phase(l, 5)

                V.tensor_copy(idxc[0:CAP, 0:1], idxT[0:CAP, 0:1]).then_inc(e_idx, 1)

                def expert(l, e, p):
                    done = l * EXPERTS + e
                    rnd = l * ROUNDS + 3 + e
                    dve.wait_ge(rows_added, done + CREDIT)
                    V.tensor_copy(gatec[0:CAP, :], gateT[0:CAP, bass.ds(e, 1)])
                    V.tensor_copy(idxc[0:CAP, 1 - p:2 - p], idxT[0:CAP, bass.ds(e + 1, 1)]).then_inc(e_idx, 1)

                    def hidden(c):
                        dve.wait_ge(e_sil, 2 * done + 1 + c + CREDIT)
                        V.tensor_tensor(hid[0:CAP, c * 512:(c + 1) * 512], sil[0:CAP, c * 512:(c + 1) * 512],
                                        PS[0:CAP, 2 + c, :], ALU.mult).then_inc(e_hid, 1)

                    def take_hidden(c, turned, done_sem):
                        dve.wait_ge(turned, done + 1)
                        V.tensor_copy(hidT[:, 4 * c:4 * c + 4, :].rearrange("p j n -> p (j n)"),
                                      PS[:, 6 + c, 0:4 * CAP]).then_inc(done_sem, 1)

                    dve.wait_ge(e_U0, done + 1)
                    hidden(0)
                    take_hidden(0, e_T0, e_hT0)
                    dve.wait_ge(slot_used[3], rnd + 1 + CREDIT)
                    hidden(1)
                    take_hidden(1, e_T1, e_hT1)
                    dve.wait_ge(slot_used[5], rnd + 1 + CREDIT)
                    V.scalar_tensor_tensor(yb[0:CAP, :], pair(4)[0:CAP, :], gatec[0:CAP, :], g2b[0:CAP, :],
                                           ALU.mult, ALU.mult).then_inc(e_y, 1)

                with dve.Fori(0, EXPERTS // 2) as e2:
                    expert(l, 2 * e2, 0)
                    expert(l, 2 * e2 + 1, 1)
                finish_phase(l, 6)
            assert chain[0] == V_LINKS, ("V_LINKS", chain[0])

            dve.wait_ge(fin_g, 16)
            for t in range(NT):
                dve.wait_ge(fin_r, t + 1)
                V.scalar_tensor_tensor(xf[:, t, :], xf[:, t, :], stat[:, 24 + t:25 + t], fgb,
                                       ALU.mult, ALU.mult).then_inc(fin_y, 1)

        @block.gpsimd
        def _(pool):
            G = nc.gpsimd
            pool.sem_inc(rows_added, CREDIT)
            chain = [0, 0]

            def reach(semaphore, value):
                wait_apart(pool, semaphore, value)

            def link(ins_):
                chain[0] += 1
                ins_.then_inc(pool_chain, 1)
                reach(pool_chain, chain[1] + chain[0])

            def finish_phase(l, k):
                pool.drain().then_inc(phase_done, 1)
                reach(phase_done, 4 * (l * PHASES + k))

            def rsqrt_mean(out, sums, n, count, done):
                link(G.tensor_scalar(out, sums, 1.0 / count, EPS, ALU.mult, ALU.add))
                G.tensor_tensor(out, out, neghalf[:, :].to_broadcast([P, n]), ALU.pow).then_inc(done, 1)

            G.memset(mean_w[:, :], 1.0 / 256).then_inc(consts_set, 1)
            G.memset(pool_w[:, :, :], 0.0).then_inc(consts_set, 1)
            G.memset(scT[:, :, :], 0.0).then_inc(consts_set, 1)
            reach(const_loaded, 16 * N_CONST)

            with pool.Fori(0, LAYERS) as l:
                chain[0], chain[1] = 0, l * G_LINKS
                finish_phase(l, 1)

                for i, lo, hi in ((0, 0, PAD), (0, PAD + LAT, CTX0), (0, CTX0 + CTX, SEQW)):
                    G.memset(poolT[:, :, lo:hi], 0.0)
                    last = G.memset(u[:, :, lo:hi], 0.0)
                last.then_inc(pads_zero, 1)

                def norm_stat(l, t):
                    reach(n_ss, NT * l + t + 1)
                    rsqrt_mean(stat[:, 24 + t:25 + t], stat[:, t:t + 1], 1, D, n_rstd)

                def step_j(l, t):
                    reach(p_ms, NT * l + t + 1)
                    if t >= 1:
                        reach(p_qs, NT * l + t)
                    rsqrt_mean(stat[:, 38:44], stat[:, 32:38], 6, HD, p_r)
                    if t == LT:
                        return
                    reach(p_ds, NT * l + t + 1)
                    st = stage[:, t % 2, 384:896]
                    x4 = st.rearrange("p (h d two) -> p h d two", h=16, two=2)
                    s4 = rd2.rearrange("p (h d two) -> p h d two", h=16, two=2)
                    ts = rope_d[:, t, 1, :].rearrange("p (d two) -> p d two", two=2)
                    G.tensor_tensor(rd1.rearrange("p (h d) -> p h d", h=16), st.rearrange("p (h d) -> p h d", h=16),
                                    rope_d[:, t, 0, :].unsqueeze(1).to_broadcast([P, 16, 32]), ALU.mult)
                    for a in range(2):
                        fin = G.tensor_tensor(s4[:, :, :, a], x4[:, :, :, 1 - a],
                                              ts[:, :, a].unsqueeze(1).to_broadcast([P, 16, 16]), ALU.mult)
                    link(fin)
                    G.tensor_tensor(st, rd1, rd2, ALU.add).then_inc(rd_done, 1)

                norm_stat(l, 0)
                norm_stat(l, 1)
                for kind, n in TAKE_ORDER:
                    if kind == "s":
                        norm_stat(l, n)
                    elif kind == "j":
                        step_j(l, n)
                finish_phase(l, 2)

                def spread(l, g):
                    t, r = divmod(g, 3)
                    if g >= SPREAD_BUFS:
                        reach(t_scores, NM * l + 4 * (g - SPREAD_BUFS + 1))
                    rows = slice(t * P, (t + 1) * P)
                    out = spread_queries(g)
                    if r == 0:
                        for half in range(2):
                            last = G.tensor_tensor(out[:, 2 * half:2 * half + 2, :], qkT[:, 0:2, rows],
                                                   rows_of[:, 4 + half:5 + half].unsqueeze(2).to_broadcast([P, 2, P]),
                                                   ALU.mult)
                    else:
                        last = G.tensor_tensor(out, qkT[:, 2 + r, rows].unsqueeze(1).to_broadcast([P, 4, P]),
                                               rows_of[:, 0:4].unsqueeze(2).to_broadcast([P, 4, P]), ALU.mult)
                    last.then_inc(q_spread, 1)

                for g in range(SPREAD_BUFS):
                    spread(l, g)

                reach(pads_zero, l + 1)
                half = slice(HD, P)
                for i in range(2):
                    x = poolT[:, i, :]
                    link(G.tensor_tensor(wa[:, 1:SEQW], x[:, 0:SEQW - 1], x[:, 1:SEQW], ALU.add))
                    if i == 0:
                        link(G.tensor_tensor(wb[half, 2:SEQW - 1], wa[half, 1:SEQW - 2], wa[half, 3:SEQW], ALU.add))
                    else:
                        link(G.tensor_tensor(wb[:, 2:SEQW - 1], wa[:, 1:SEQW - 2], wa[:, 3:SEQW], ALU.add))
                        link(G.tensor_tensor(wa[:, 4:SEQW - 3], wb[:, 2:SEQW - 5], wb[:, 6:SEQW - 1], ALU.add))
                        link(G.tensor_tensor(wb[half, 8:SEQW - 7], wa[half, 4:SEQW - 11], wa[half, 12:SEQW - 3],
                                             ALU.add))
                    for rows, src in ((slice(0, HD), wa), (half, wb)):
                        last = G.tensor_scalar(poolD3[rows, i, :], src[rows, PAD:PAD + OUTW], invw[rows, i:i + 1],
                                               None, ALU.mult)
                    link(last)
                    for c0, n in ((0, LAT), (CTX0 - PAD, CTX)):
                        for side in range(2):
                            c = c0 + side * (n - 8)
                            ends = poolD3[:, i, c:c + 8]
                            last = G.tensor_tensor(ends, ends, edge[:, i, side, :], ALU.mult)
                    link(last)
                    link(G.tensor_tensor(poolD3[:, i, :], poolD3[:, i, :], x[:, PAD:PAD + OUTW], ALU.subtract))

                own = list(range(DVE_TAPS, TAPS))
                for t in range(NT):
                    for g in range(SPREAD_BUFS + 3 * t, min(SPREAD_BUFS + 3 * t + 3, SPREADS)):
                        spread(l, g)
                    reach(t_dss, NT * l + t + 1)
                    rsqrt_mean(stat[:, 56:60], stat[:, 52:56], 4, HD, t_dr)
                    for k in own[4 * t:4 * t + 4]:
                        if k == DVE_TAPS:
                            link(G.tensor_scalar(wb[:, 0:OUTW], u[:, 1, k:k + OUTW], cwT[:, 1, k:k + 1], None,
                                                 ALU.mult))
                        else:
                            link(G.tensor_scalar(tap, u[:, 1, k:k + OUTW], cwT[:, 1, k:k + 1], None, ALU.mult))
                            link(G.tensor_tensor(wb[:, 0:OUTW], wb[:, 0:OUTW], tap, ALU.add))
                finish_phase(l, 3)

                finish_phase(l, 4)

                for t in range(NT):
                    reach(o_ss, NT * l + t + 1)
                    rsqrt_mean(stat[:, 24 + t:25 + t], stat[:, 16 + t:17 + t], 1, D, o_r)
                finish_phase(l, 5)

                def gather(p):
                    pool.indirect_dma_start(xg[0:CAP, p, :], None, xn_dram[:, :],
                                            bass.IndirectOffsetOnAxis(ap=idxc[0:CAP, p:p + 1], axis=0))\
                        .then_inc(e_gath[p], 16)

                reach(e_idx, 17 * l + 1)
                gather(0)

                def expert(l, e, p):
                    done = l * EXPERTS + e
                    reach(e_idx, 17 * l + e + 2)
                    reach(e_X1, 17 * l + e + 1)
                    gather(1 - p)
                    reach(e_y, done + 1 + CREDIT)
                    pool.indirect_dma_start(x_dram[:, :], bass.IndirectOffsetOnAxis(ap=idxc[0:CAP, p:p + 1], axis=0),
                                            yb[0:CAP, :], None, compute_op=ALU.add).then_inc(e_scat, 16)
                    pool.wait_ge(e_scat, 16 * (done + 1))
                    pool.sem_inc(rows_added, 1)

                with pool.Fori(0, EXPERTS // 2) as e2:
                    expert(l, 2 * e2, 0)
                    expert(l, 2 * e2 + 1, 1)
                finish_phase(l, 6)
            assert chain[0] == G_LINKS, ("G_LINKS", chain[0])

            for t in range(NT):
                reach(fin_ss, t + 1)
                last = rsqrt_mean(stat[:, 24 + t:25 + t], stat[:, 16 + t:17 + t], 1, D, fin_r)


V_LINKS = 169
G_LINKS = 65
ORDER = (("x", 0), ("s", 2), ("x", 1), ("j", 0), ("s", 3), ("x", 2), ("j", 1), ("q", 0), ("s", 4), ("x", 3), ("j", 2),
         ("q", 1), ("x", 4), ("j", 3), ("q", 2), ("j", 4), ("q", 3), ("f", 0), ("q", 4), ("f", 1), ("f", 2),
         ("f", 3), ("f", 4), ("f", 5))
TAKE_ORDER = (("x", 0), ("s", 2), ("x", 1), ("x", 2), ("j", 0), ("s", 3), ("q", 0), ("x", 3), ("j", 1), ("s", 4),
              ("q", 1), ("x", 4), ("j", 2), ("q", 2), ("j", 3), ("q", 3), ("j", 4), ("f", 0), ("q", 4), ("f", 1),
              ("f", 2), ("f", 3), ("f", 4), ("f", 5))
assert sorted(TAKE_ORDER) == sorted(ORDER)
_BANK_USES = [step for step in ORDER if step[0] in "xq"]
XUSE = {n: i for i, (kind, n) in enumerate(_BANK_USES) if kind == "x"}
FCHUNK = ((0, 512), (0, 640), (2, 0), (0, 768), (2, 128), (0, 896))


def shape_constants():
    f = np.float32

    def rope(dim):
        rows = np.repeat(np.arange(8), 64).astype(f)
        cols = np.tile(np.arange(64), 8).astype(f)
        quarter = dim // 4
        inv = f(10000.0) ** (-np.arange(quarter, dtype=f) / f(quarter))
        ang = np.concatenate([rows[:, None] * inv, cols[:, None] * inv], axis=-1)
        c, s = np.cos(ang).astype(f), np.sin(ang).astype(f)
        both = np.empty((512, 2, dim), f)
        both[:, 0, 0::2], both[:, 0, 1::2] = c, c
        both[:, 1, 0::2], both[:, 1, 1::2] = -s, s
        return both

    edge, invw = np.ones((128, 2, 2, 8), f), np.empty((128, 2), f)
    for g, w in enumerate((2, 4, 8, 16)):
        rows = slice(64 * (g % 2), 64 * (g % 2) + 64)
        invw[rows, g // 2] = 1.0 / w
        for t in range(8):
            edge[rows, g // 2, 0, t] = w / (min(t, w // 2) + w - w // 2)
            edge[rows, g // 2, 1, t] = w / (w // 2 + min(w - w // 2, 8 - t))
    rows_of = np.concatenate([np.repeat(np.eye(4), 32, axis=0), np.repeat(np.eye(2), 64, axis=0)], axis=1).astype(f)
    lam = [0.8 - 0.6 * float(np.exp(-0.3 * n)) for n in range(2)]
    return {"k_ident": np.eye(128, dtype=f), "k_rope_a": rope(64), "k_rope_d": rope(32), "k_edge": edge,
            "k_invw": invw, "k_rows_of": rows_of, "k_neghalf": np.full((128, 1), -0.5, f),
            "k_lam": np.array([[x, 1.0 - x] for x in lam], f)}


_OUTS = {"y_prompt": (1, 128, 1024), "y_sample": (1, 512, 1024), "state_gqa_k": (1, 2, 128, 2, 64),
         "state_gqa_v": (1, 2, 128, 2, 64), "state_diff_k": (1, 2, 128, 4, 64), "state_diff_v": (1, 2, 128, 4, 64)}


def kernel(**inputs):
    import concourse.bacc as _bacc
    from concourse.bass_utils import run_bass_kernel_spmd as _run

    nc = _bacc.Bacc("TRN2", target_bir_lowering=False, num_devices=1)
    arrays, ins, outs = {}, {}, {}
    for name, a in {**inputs, **shape_constants()}.items():
        a = np.ascontiguousarray(a)
        arrays[f"in_{name}"] = a
        ins[name] = nc.dram_tensor(f"in_{name}", a.shape, mybir.dt.from_np(a.dtype), kind="ExternalInput").ap()
    for name, shape in _OUTS.items():
        outs[name] = nc.dram_tensor(f"out_{name}", shape, mybir.dt.float32, kind="ExternalOutput").ap()
    backbone_step_kernel(nc, ins, outs)
    r = _run(nc, [arrays], core_ids=[0])
    return tuple(r.results[0][f"out_{name}"] for name in _OUTS)
```
